# Optimizing a Trainium2 kernel written in Bass

```python
import math
import jax, jax.numpy as jnp
from jax import lax
import numpy as np

D_MODEL = 1024
BATCH = 1
SEQ = 256
DEPTH = 2

HEAD_DIM = 64
MOBA_HEADS = 8
MOBA_WIDTH = MOBA_HEADS * HEAD_DIM
MOBA_BLOCK = 256
MOBA_TOPK = 3
MOBA_QCHUNK = 128
RWKV_HEADS = 8
RWKV_WIDTH = RWKV_HEADS * HEAD_DIM
DECAY_LORA = 64
ICLR_LORA = 64
GN_EPS = HEAD_DIM * 1e-5
DECAY_SCALE = math.exp(-0.5)
SWA_Q_HEADS = 8
SWA_KV_HEADS = 2
SWA_GROUP = SWA_Q_HEADS // SWA_KV_HEADS
SWA_WIDTH = SWA_Q_HEADS * HEAD_DIM
SWA_KV_WIDTH = SWA_KV_HEADS * HEAD_DIM
WINDOW = 128
SWA_BLOCK = 128
ROPE_THETA = 10000.0
LN_EPS = 1e-5
ALPHA = (2 * DEPTH) ** 0.25
BETA = (8 * DEPTH) ** -0.25

A_SPLITS = (MOBA_WIDTH, MOBA_WIDTH, MOBA_WIDTH, MOBA_WIDTH)
B_SPLITS = (RWKV_WIDTH, RWKV_WIDTH, RWKV_WIDTH, DECAY_LORA, ICLR_LORA, RWKV_WIDTH)
C_SPLITS = (SWA_WIDTH, SWA_KV_WIDTH, SWA_KV_WIDTH, SWA_WIDTH)
G_SPLITS = (D_MODEL, D_MODEL, D_MODEL)
GROUP_SPLITS = (sum(A_SPLITS), sum(B_SPLITS), sum(C_SPLITS), sum(G_SPLITS))
IN_WIDTH = sum(GROUP_SPLITS)
RWKV_IN_WIDTH = sum(B_SPLITS)

kernel_name = 'hybrid_moba_rwkv7_swa_sink_gated'

def _split(h, sizes):
    offs = np.cumsum(sizes)[:-1].tolist()
    return jnp.split(h, offs, axis=-1)

def layer_norm(x, g, b):
    xf = x.astype(jnp.float32)
    mu = xf.mean(-1, keepdims=True)
    var = jnp.square(xf - mu).mean(-1, keepdims=True)
    return ((xf - mu) * lax.rsqrt(var + LN_EPS) * g.astype(jnp.float32) + b.astype(jnp.float32)).astype(x.dtype)

def rope(x, positions):
    half = HEAD_DIM // 2
    inv = jnp.power(ROPE_THETA, -jnp.arange(half, dtype=jnp.float32) / half)
    ang = positions.astype(jnp.float32)[..., None] * inv
    cos = jnp.cos(ang)[:, :, None, :]
    sin = jnp.sin(ang)[:, :, None, :]
    xf = x.astype(jnp.float32)
    x1, x2 = xf[..., :half], xf[..., half:]
    return jnp.concatenate([x1 * cos - x2 * sin, x2 * cos + x1 * sin], axis=-1).astype(x.dtype)

def moba_attention(q, k, v):
    B, S, H, D = q.shape
    s_pad = -(-S // MOBA_BLOCK) * MOBA_BLOCK
    nb = s_pad // MOBA_BLOCK
    topk = min(MOBA_TOPK, nb)
    pad = ((0, 0), (0, s_pad - S), (0, 0), (0, 0))
    kb = jnp.pad(k, pad).reshape(B, nb, MOBA_BLOCK, H, D).transpose(0, 3, 1, 2, 4)
    vb = jnp.pad(v, pad).reshape(B, nb, MOBA_BLOCK, H, D).transpose(0, 3, 1, 2, 4)
    kmean = kb.astype(jnp.float32).mean(axis=3)
    qh = q.transpose(0, 2, 1, 3)
    bi = jnp.arange(B)[:, None, None, None]
    hi = jnp.arange(H)[None, :, None, None]
    blk_ids = jnp.arange(nb)
    offs = jnp.arange(MOBA_BLOCK)
    scale = D ** -0.5

    def chunk(c):
        q0 = c * MOBA_QCHUNK
        qc = lax.dynamic_slice_in_dim(qh, q0, MOBA_QCHUNK, axis=2)
        qpos = q0 + jnp.arange(MOBA_QCHUNK)
        own = q0 // MOBA_BLOCK
        gate = jnp.einsum('bhqd,bhnd->bhqn', qc.astype(jnp.float32), kmean)
        gate = jnp.where(blk_ids < own, gate, -jnp.inf)
        _, idx = lax.top_k(gate, topk)
        valid = idx < own
        ksel = kb[bi, hi, idx]
        vsel = vb[bi, hi, idx]
        s_sel = jnp.einsum('bhqd,bhqnkd->bhqnk', qc, ksel).astype(jnp.float32) * scale
        s_sel = jnp.where(valid[..., None], s_sel, -jnp.inf).reshape(B, H, MOBA_QCHUNK, topk * MOBA_BLOCK)
        kown = lax.dynamic_index_in_dim(kb, own, axis=2, keepdims=False)
        vown = lax.dynamic_index_in_dim(vb, own, axis=2, keepdims=False)
        s_own = jnp.einsum('bhqd,bhkd->bhqk', qc, kown).astype(jnp.float32) * scale
        kpos = own * MOBA_BLOCK + offs
        s_own = jnp.where(kpos[None, :] <= qpos[:, None], s_own, -jnp.inf)
        p = jax.nn.softmax(jnp.concatenate([s_sel, s_own], axis=-1), axis=-1).astype(v.dtype)
        p_sel = p[..., :topk * MOBA_BLOCK].reshape(B, H, MOBA_QCHUNK, topk, MOBA_BLOCK)
        p_own = p[..., topk * MOBA_BLOCK:]
        return (jnp.einsum('bhqnk,bhqnkd->bhqd', p_sel, vsel)
                + jnp.einsum('bhqk,bhkd->bhqd', p_own, vown))

    out = lax.map(chunk, jnp.arange(S // MOBA_QCHUNK))
    return out.transpose(1, 0, 3, 2, 4).reshape(B, S, H * D)

def swa_sink_attention(q, k, v, sinks):
    B, S, _, D = q.shape
    nb = S // SWA_BLOCK
    qb = q.reshape(B, nb, SWA_BLOCK, SWA_KV_HEADS, SWA_GROUP, D)
    pad = ((0, 0), (SWA_BLOCK, 0), (0, 0), (0, 0))
    kp = jnp.pad(k, pad).reshape(B, nb + 1, SWA_BLOCK, SWA_KV_HEADS, D)
    vp = jnp.pad(v, pad).reshape(B, nb + 1, SWA_BLOCK, SWA_KV_HEADS, D)
    kband = jnp.concatenate([kp[:, :-1], kp[:, 1:]], axis=2)
    vband = jnp.concatenate([vp[:, :-1], vp[:, 1:]], axis=2)
    s = jnp.einsum('bnqhgd,bnkhd->bnhgqk', qb, kband).astype(jnp.float32) * (D ** -0.5)
    qi = jnp.arange(SWA_BLOCK)[:, None]
    ki = jnp.arange(2 * SWA_BLOCK)[None, :] - SWA_BLOCK
    rel = qi - ki
    kabs = jnp.arange(nb)[:, None, None] * SWA_BLOCK + ki[None]
    mask = (rel >= 0)[None] & (rel < WINDOW)[None] & (kabs >= 0)
    s = jnp.where(mask[None, :, None, None], s, -jnp.inf)
    sink = sinks.astype(jnp.float32).reshape(SWA_KV_HEADS, SWA_GROUP)[None, None, :, :, None, None]
    m = jnp.maximum(s.max(-1, keepdims=True), sink)
    p = jnp.exp(s - m)
    denom = p.sum(-1, keepdims=True) + jnp.exp(sink - m)
    o = jnp.einsum('bnhgqk,bnkhd->bnqhgd', (p / denom).astype(v.dtype), vband)
    return o.reshape(B, S, SWA_Q_HEADS * D)

def rwkv7_time_mix(r, k, v, w_lo, a_lo, w0, w_up, a0, a_up, k_k, k_a, r_k, gn_g, gn_b):
    B, S, _ = r.shape
    H, D = RWKV_HEADS, HEAD_DIM
    f = lambda t: t.astype(jnp.float32)
    r, k, v, w_lo, a_lo = f(r), f(k), f(v), f(w_lo), f(a_lo)
    decay = jnp.exp(-DECAY_SCALE * jax.nn.sigmoid(f(w0) + jnp.tanh(w_lo) @ f(w_up)))
    a = jax.nn.sigmoid(f(a0) + a_lo @ f(a_up))
    kk = (k * f(k_k)).reshape(B, S, H, D)
    kk = kk / jnp.maximum(jnp.sqrt(jnp.sum(kk * kk, -1, keepdims=True)), 1e-12)
    k = k * (1.0 + (a - 1.0) * f(k_a))
    hd = lambda t: t.reshape(B, S, H, D)
    r4, k4, v4, w4, a4 = hd(r), hd(k), hd(v), hd(decay), hd(a)
    xs = tuple(jnp.moveaxis(t, 1, 0) for t in (r4, w4, k4, v4, kk, a4))

    def step(state, inp):
        r_t, w_t, k_t, v_t, kk_t, a_t = inp
        sa = jnp.einsum('bhvk,bhk->bhv', state, -kk_t)
        state = (state * w_t[:, :, None, :]
                 + sa[..., None] * (kk_t * a_t)[:, :, None, :]
                 + v_t[..., None] * k_t[:, :, None, :])
        return state, jnp.einsum('bhvk,bhk->bhv', state, r_t)

    state0 = jnp.zeros((B, H, D, D), jnp.float32)
    _, y = lax.scan(step, state0, xs)
    y = jnp.moveaxis(y, 0, 1)
    mu = y.mean(-1, keepdims=True)
    var = jnp.square(y - mu).mean(-1, keepdims=True)
    y = ((y - mu) * lax.rsqrt(var + GN_EPS)).reshape(B, S, H * D) * f(gn_g) + f(gn_b)
    bonus = (jnp.sum(r4 * k4 * f(r_k), -1, keepdims=True) * v4).reshape(B, S, H * D)
    return y + bonus

def hybrid_layer(x, positions, w_in, mu_rwkv, w0, w_up, a0, a_up, k_k, k_a, r_k,
                 gn_g, gn_b, sinks, w_branch_a, w_branch_b, w_branch_c, w_out, ln_g, ln_b):
    B, S, _ = x.shape
    h = x @ w_in
    hA, hB, hC, hG = _split(h, GROUP_SPLITS)
    qa, ka, va, za = _split(hA, A_SPLITS)
    qa = rope(qa.reshape(B, S, MOBA_HEADS, HEAD_DIM), positions)
    ka = rope(ka.reshape(B, S, MOBA_HEADS, HEAD_DIM), positions)
    oa = moba_attention(qa, ka, va.reshape(B, S, MOBA_HEADS, HEAD_DIM))
    hB_prev = jnp.pad(hB, ((0, 0), (1, 0), (0, 0)))[:, :S]
    hB = hB + (hB_prev - hB) * mu_rwkv
    rb, kb, vb, wlo, alo, zb = _split(hB, B_SPLITS)
    ob = rwkv7_time_mix(rb, kb, vb, wlo, alo, w0, w_up, a0, a_up, k_k, k_a, r_k, gn_g, gn_b).astype(x.dtype)
    qc, kc, vc, zc = _split(hC, C_SPLITS)
    qc = rope(qc.reshape(B, S, SWA_Q_HEADS, HEAD_DIM), positions)
    kc = rope(kc.reshape(B, S, SWA_KV_HEADS, HEAD_DIM), positions)
    oc = swa_sink_attention(qc, kc, vc.reshape(B, S, SWA_KV_HEADS, HEAD_DIM), sinks)
    ga, gb, gc = _split(hG, G_SPLITS)
    ya = (oa * jax.nn.silu(za)) @ w_branch_a
    yb = (ob * jax.nn.silu(zb)) @ w_branch_b
    yc = (oc * jax.nn.silu(zc)) @ w_branch_c
    merged = jax.nn.sigmoid(ga) * ya + jax.nn.sigmoid(gb) * yb + jax.nn.sigmoid(gc) * yc
    out = merged @ w_out
    return layer_norm(ALPHA * x + out, ln_g, ln_b)

def setup_inputs(seed: int = 0) -> dict:
    key = jax.random.key(seed)
    ks = jax.random.split(key, 24)
    L = DEPTH
    nrm = lambda k, shape, s: jax.random.normal(k, shape, jnp.float32) * s
    x = jax.random.normal(ks[0], (BATCH, SEQ, D_MODEL), jnp.float32)
    positions = jnp.broadcast_to(jnp.arange(SEQ, dtype=jnp.int32)[None, :], (BATCH, SEQ))
    return {
        'x': x,
        'positions': positions,
        'w_in': nrm(ks[1], (L, D_MODEL, IN_WIDTH), D_MODEL ** -0.5),
        'mu_rwkv': jax.random.uniform(ks[2], (L, RWKV_IN_WIDTH), jnp.float32),
        'w0': nrm(ks[3], (L, RWKV_WIDTH), 1.0),
        'w_up': nrm(ks[4], (L, DECAY_LORA, RWKV_WIDTH), 0.5 * DECAY_LORA ** -0.5),
        'a0': nrm(ks[5], (L, RWKV_WIDTH), 0.5),
        'a_up': nrm(ks[6], (L, ICLR_LORA, RWKV_WIDTH), 0.5 * ICLR_LORA ** -0.5),
        'k_k': 0.85 + nrm(ks[7], (L, RWKV_WIDTH), 0.05),
        'k_a': 1.0 + nrm(ks[8], (L, RWKV_WIDTH), 0.05),
        'r_k': nrm(ks[9], (L, RWKV_HEADS, HEAD_DIM), 0.1),
        'gn_g': 1.0 + nrm(ks[10], (L, RWKV_WIDTH), 0.05),
        'gn_b': nrm(ks[11], (L, RWKV_WIDTH), 0.01),
        'sinks': nrm(ks[12], (L, SWA_Q_HEADS), 1.0),
        'w_branch_a': nrm(ks[13], (L, MOBA_WIDTH, D_MODEL), BETA * MOBA_WIDTH ** -0.5),
        'w_branch_b': nrm(ks[14], (L, RWKV_WIDTH, D_MODEL), BETA * RWKV_WIDTH ** -0.5),
        'w_branch_c': nrm(ks[15], (L, SWA_WIDTH, D_MODEL), BETA * SWA_WIDTH ** -0.5),
        'w_out': nrm(ks[16], (L, D_MODEL, D_MODEL), BETA * D_MODEL ** -0.5),
        'ln_g': 1.0 + nrm(ks[17], (L, D_MODEL), 0.05),
        'ln_b': nrm(ks[18], (L, D_MODEL), 0.01),
    }

def reference(x, positions, w_in, mu_rwkv, w0, w_up, a0, a_up, k_k, k_a, r_k,
              gn_g, gn_b, sinks, w_branch_a, w_branch_b, w_branch_c, w_out, ln_g, ln_b):
    for l in range(DEPTH):
        x = hybrid_layer(x, positions, w_in[l], mu_rwkv[l], w0[l], w_up[l], a0[l], a_up[l],
                         k_k[l], k_a[l], r_k[l], gn_g[l], gn_b[l], sinks[l],
                         w_branch_a[l], w_branch_b[l], w_branch_c[l], w_out[l], ln_g[l], ln_b[l])
    return x


_drawn_inputs = setup_inputs


def setup_inputs(seed=0):
    import zlib

    import numpy as np

    out = dict(_drawn_inputs(seed))
    spreads = {}
    factors = {'w_up': 8.0,
     'a0': 3.396,
     'a_up': 4.314,
     'k_k': 58.789,
     'k_a': 8.0,
     'r_k': 3.877,
     'gn_g': 8.0,
     'gn_b': 64.0,
     'sinks': 8.0,
     'w_branch_a': 3.217,
     'w_branch_c': 3.332,
     'ln_b': 4.082}
    for name, (base, spread) in spreads.items():
        noise = np.random.default_rng([zlib.crc32(name.encode()), seed]).standard_normal(out[name].shape)
        drawn = base * np.exp(spread * noise) if base else spread * noise
        out[name] = __import__('jax').numpy.asarray(drawn.astype(out[name].dtype))
    for name, factor in factors.items():
        out[name] = (out[name] * factor).astype(out[name].dtype)
    return out
```

```python
import math
from contextlib import ExitStack

import numpy as np

import concourse.bass as bass
from concourse import mybir

P = 128
D = 1024
SEQ = 256
DEPTH = 2
HD = 64
H = 8
W5 = 512
KT = D // P
ALPHA = (2 * DEPTH) ** 0.25
DECAY_SCALE = math.exp(-0.5)
GN_EPS = HD * 1e-5
LN_EPS = 1e-5
SCALE = HD ** -0.5
CH = 64
NC = SEQ // CH
NVEC = 17 + 28
RAW, SPL = 4, 4
ROUND = 1.5 * 2.0 ** 23
TWO_PI = (6.28125, 0.0019350051879882812, 2 * math.pi - 6.28125 - 0.0019350051879882812)
PI_MAX = 3.1415925
INPUTS = ("x", "positions", "w_in", "mu_rwkv", "w0", "w_up", "a0", "a_up", "k_k", "k_a", "r_k", "gn_g", "gn_b", "sinks",
          "w_branch_a", "w_branch_b", "w_branch_c", "w_out", "ln_g", "ln_b", "consts")
LEAD = 3

C_ID, C_BO, C_CEN = 0, 128, 256
C_MSK = 384
C_M16, C_M32 = 512, 576
C_RST = 640
C_INV = C_RST + SEQ
C_SEL2 = C_INV + 32
C_SEL8 = C_SEL2 + 2
C_EYE16 = C_SEL8 + 512
C_NEG = C_EYE16 + 256
C_ALL = C_NEG + 256

UNITS = [
    ("lora", "T", "w_in", 3584, 128, 8), ("r", "T", "w_in", 2048, W5, 8), ("k", "T", "w_in", 2560, W5, 8),
    ("v", "T", "w_in", 3072, W5, 8), ("Aq", "N", "w_in", 0, W5, 8), ("Ak", "N", "w_in", 512, W5, 8),
    ("Av", "N", "w_in", 1024, W5, 8), ("Cq", "N", "w_in", 4224, W5, 8), ("Ckv", "N", "w_in", 4736, 256, 8),
    ("zA", "T", "w_in", 1536, W5, 8), ("GA0", "N", "w_in", 5504, W5, 8), ("GA1", "N", "w_in", 6016, W5, 8),
    ("bA0", "N", "w_branch_a", 0, W5, 4), ("bA1", "N", "w_branch_a", 512, W5, 4),
    ("zC", "T", "w_in", 4992, W5, 8), ("GC0", "N", "w_in", 7552, W5, 8), ("GC1", "N", "w_in", 8064, W5, 8),
    ("bC0", "N", "w_branch_c", 0, W5, 4), ("bC1", "N", "w_branch_c", 512, W5, 4),
    ("zB", "T", "w_in", 3712, W5, 8), ("GB0", "N", "w_in", 6528, W5, 8), ("GB1", "N", "w_in", 7040, W5, 8),
    ("bB0", "N", "w_branch_b", 0, W5, 4), ("bB1", "N", "w_branch_b", 512, W5, 4),
    ("o0", "N", "w_out", 0, W5, 8), ("o1", "N", "w_out", 512, W5, 8),
]
UIDX = {u[0]: i for i, u in enumerate(UNITS)}
TILES = []
for _u, (_n, _lay, _src, _c, _w, _k) in enumerate(UNITS):
    _step = {128: 4, 256: 4, W5: 2}[_w]
    TILES += [(_u, _k0, _step) for _k0 in range(0, _k, _step)]
NT = len(TILES)
assert NT % RAW == 0 and NT % SPL == 0 and len(UNITS) % 2 == 0
LAST = {u: max(n for n, t in enumerate(TILES) if t[0] == u) for u in range(len(UNITS))}

def _attn(x, g0):
    out = []
    for g in range(6):
        out += [(g0 + 2 * g, "sc", x, g), (g0 + 2 * g + 2, "pt", x, g), (g0 + 2 * g + 3, "pv", x, g)]
    return out + [(g0 + 7, "ot", x, 0), (g0 + 15, "ot", x, 1)]


MIXED = ("lora", "r", "k", "v", "zB")
WORK = [(-1, "xt", t, h) for t in range(2) for h in range(2)] + [(-1, "vec")]
WORK += [(3, "dec", i) for i in range(2)] + [(3, "icl", i) for i in range(2)]
WORK += [(10, "nss", "k"), (12, "nrt", "k"), (13, "nrb", "k", 0), (13, "nrb", "k", 1)]
WORK += [(14, "vt", 0), (14, "vt", 1)]
WORK += [(19, "qt", "Aq", 0), (19, "qt", "Aq", 1), (23, "qt", "Ak", 0), (23, "qt", "Ak", 1)]
WORK += _attn("A", 24) + [(22, "bon", 0), (22, "bon", 1)]
WORK += [(23 + i, "rs", i // 4, (i % 4) // 2, i % 2) for i in range(8)]
WORK += [(36, "qt", "Cq", 0), (36, "qt", "Cq", 1), (37, "qt", "Ck", 0), (37, "qt", "Ck", 1)] + _attn("C", 38)
for _i, (_c, _t) in enumerate([(c, t) for c in range(2) for t in range(2)]):
    WORK += [(41 + _i // 2, "w1", _c, _t), (44 + _i // 2, "t1", _c, _t), (46 + _i // 2, "tt1", _c, _t),
             (48 + _i // 2, "w2", _c, _t), (51 + _i // 2, "tt2", _c, _t)]
WORK += [(53, "bt", "b", 0), (53, "bt", "b", 1), (54, "bt", "k", 0), (54, "bt", "k", 1)]
for _c in range(NC):
    WORK += [(54 + 3 * _c, "cp", _c), (55 + 3 * _c, "cu", _c), (56 + 3 * _c, "cy", _c)]
    WORK += [(56 + 3 * _c, "cs", _c)] if _c < NC - 1 else []
WORK += [(67, "cen", 0), (67, "cen", 1), (68, "nss", "y"), (70, "nrt", "y"), (71, "nrb", "y", 0), (71, "nrb", "y", 1)]
WORK += [(79, "mt", t, h) for t in range(2) for h in range(2)]
WORK = [w for _, w in sorted(enumerate(WORK), key=lambda e: (e[1][0], e[0]))]
GAP = {w[1:]: w[0] for w in WORK}
WIDX = {w[1:]: i for i, w in enumerate(WORK)}


def release(w):
    kind = w[0]
    renamed = {"xt": "xtl", "mt": "mtl", "sc": "exp"}
    on_act = ("vec", "dec", "icl", "nrt", "vt", "qt", "sc", "pt", "ot", "w1", "w2", "bt", "cp", "cy", "cen")
    return ("act" if kind in on_act else "dve", (renamed.get(kind, kind),) + w[1:])


def unit_release(name):
    if name in MIXED:
        return "dve", ("shift", name)
    if name in ("Aq", "Ak", "Cq"):
        return "dve", ("rope", name, 1)
    if name == "Ckv":
        return "dve", ("ropek", 1)
    if name == "Av":
        return "act", ("Av",)
    if name[0] == "z":
        return "dve", ("sz", name[1])
    if name[0] == "G":
        return "act", ("gate", name)
    return "dve", ("bmul" if name[0] == "b" else "res", name)



G_STEP = {"A": 41, "C": 55, "B": 74}


def _order(eng):
    out = []
    half = {"act": "hi", "dve": "lo"}[eng]
    out += [(-1, half, 0)] + [(-1, half, n) for n in range(1, LEAD) if eng == "act"]
    if eng == "act":
        out += [(-1, "xth", t, h) for t in range(2) for h in range(2)] + [(-1, "vec")]
    else:
        out += [(-1, "xtl", t, h) for t in range(2) for h in range(2)] + [(-1, half, n) for n in range(1, LEAD)]
        out += [(-1, "derive")]
    for n in range(NT + 1):
        if n + LEAD < NT:
            out += [(n, half, n + LEAD)]
        for u, (name, *_r) in enumerate(UNITS):
            if LAST[u] == n - 2 and name == "zB":
                out += [(n, "ztanh" if eng == "act" else "sz", "B")]
            if LAST[u] != n - 1:
                continue
            if eng == "act":
                out += [(n, "mix", name)] if name in MIXED else []
                out += [(n, "Av")] if name == "Av" else []
                out += [(n, "vc")] if name == "Ckv" else []
                out += [(n, "ztanh", name[1])] if name in ("zA", "zC") else []
                out += [(n, "gate", name)] if name[0] == "G" else []
                out += [(n, "ltanh")] if name == "lora" else []
                out += [(n, "ksq")] if name == "k" else []
            else:
                out += [(n, "shift", name)] if name in MIXED else []
                out += [(n, "rope", name, t) for t in range(2)] if name in ("Aq", "Ak", "Cq") else []
                out += [(n, "ropek", t) for t in range(2)] if name == "Ckv" else []
                out += [(n, "sz", name[1])] if name in ("zA", "zC") else []
                out += [(n, "bmul", name)] if name[0] == "b" else []
                out += [(n, "res", name)] if name[0] == "o" else []
        for w in WORK:
            if w[0] == n - 1 and n > 0:
                if w[1] == "sc":
                    out += [(n, "exp" if eng == "act" else "max") + w[2:]]
                elif w[1] == "mt":
                    out += [(n, "mth" if eng == "act" else "mtl") + w[2:]]
                elif release(w[1:])[0] == eng:
                    out += [(n,) + w[1:]]
        if eng == "act":
            out += [(n, "en"), (n, "ex"), (n, "ei"), (n, "ec")] if n == 8 else []
            out += [(n, "ghi", x) for x in "ACB" if G_STEP[x] == n]
        else:
            out += {5: [(n, "ld"), (n, "scan")], 9: [(n, "ta")], 15: [(n, "k2")], 16: [(n, "ara")], 17: [(n, "kb")]}.get(n, [])
            out += [(n, "sub", n - 35)] if 35 <= n < 38 else []
            out += [(n, "gn")] if n == 72 else []
            for x in "ACB":
                out += [(n, "g", x), (n, "glo", x)] if G_STEP[x] == n else []
    if eng == "dve":
        out += [(NT, "stats"), (NT, "norm", 0), (NT, "norm", 1)]
    return out


PE_ORDER = [w for w in WORK if w[0] == -1]
for _n in range(NT):
    PE_ORDER += [(_n, "tile", _n)] + [w for w in WORK if w[0] == _n]
ACT_ORDER, DVE_ORDER = _order("act"), _order("dve")
POOL_ORDER = [(0, k) for k in ("zero", "cx", "rnk", "arr", "rk", "kt", "lm1", "lm2", "states", "addC0", "addC1", "rny", "addB0", "addB1", "rstd")]
ORDER = dict(pe=PE_ORDER, act=ACT_ORDER, dve=DVE_ORDER, pool=POOL_ORDER)
PER = {e: len(o) for e, o in ORDER.items()}
NUM = {e: {w[1:]: i + 1 for i, w in enumerate(o)} for e, o in ORDER.items()}
LINKS = dict(dve=88, pool=1)


def constants():
    c = np.zeros((P, C_ALL), np.float32)
    i = np.arange(P)
    c[:, C_ID:C_ID + P] = np.eye(P)
    same = (i[:, None] // HD) == (i[None, :] // HD)
    c[:, C_BO:C_BO + P] = same
    c[:, C_CEN:C_CEN + P] = np.eye(P) - same / HD
    s, t = (i % CH)[:, None], np.arange(CH)[None, :]
    c[:, C_MSK:C_MSK + CH] = s < t
    c[:, C_MSK + CH:C_MSK + 2 * CH] = s <= t
    c[:, C_M16:C_M16 + CH] = (s // 32 == t // 32) & (s // 16 != t // 16)
    c[:, C_M32:C_M32 + CH] = s // 32 != t // 32
    c[:, C_RST:C_RST + SEQ] = (np.arange(SEQ) % CH != 0)
    half = HD // 2
    c[:, C_INV:C_INV + half] = np.power(np.float32(10000.0), -np.arange(half, dtype=np.float32) / half)
    c[:, C_SEL2] = i < HD
    c[:, C_SEL2 + 1] = i >= HD
    for j in range(4):
        for h in range(2):
            c[2 * j + h, C_SEL8 + j * P + h * HD:C_SEL8 + j * P + (h + 1) * HD] = 1
    c[:, C_EYE16:C_EYE16 + 256] = np.eye(16).reshape(-1)
    q, k = i[:, None], i[None, :]
    c[:, C_NEG:C_NEG + P] = np.where(k <= q, 0, -1e30)
    c[:, C_NEG + P:C_NEG + 2 * P] = np.where(k > q, 0, -1e30)
    return c


def hybrid_trunk(nc, x, positions, w_in, mu_rwkv, w0, w_up, a0, a_up, k_k, k_a, r_k, gn_g, gn_b, sinks,
                 w_branch_a, w_branch_b, w_branch_c, w_out, ln_g, ln_b, consts, out):
    f32, f32r, bf16, i32 = mybir.dt.float32, mybir.dt.float32r, mybir.dt.bfloat16, mybir.dt.int32
    ACT, ALU, AX = mybir.ActivationFunctionType, mybir.AluOpType, mybir.AxisListType
    weights = dict(w_in=w_in, w_branch_a=w_branch_a, w_branch_b=w_branch_b, w_branch_c=w_branch_c, w_out=w_out)

    blocks = nc.dram_tensor("blocks", (P, 256), f32, kind="Internal").ap()
    inverses = nc.dram_tensor("inverses", (P, 512), f32, kind="Internal").ap()

    with ExitStack() as ctx:
        def sb(name, cols, dt=f32, rows=P):
            return ctx.enter_context(nc.sbuf_tensor(name, [rows, cols], dt))

        raw = sb("raw", RAW * 1024)
        w_hi, w_lo = sb("w_hi", SPL * 1024, f32r), sb("w_lo", SPL * 1024, f32r)
        xres = sb("xres", 2 * D)
        xt_hi, xt_lo = sb("xt_hi", KT * SEQ, f32r), sb("xt_lo", KT * SEQ, f32r)
        g_hi, g_lo = sb("g_hi", 4 * SEQ, f32r), sb("g_lo", 4 * SEQ, f32r)
        o_A, o_C = sb("o_A", 4 * SEQ), sb("o_C", 4 * SEQ)
        gate, merged, sz, tmp = sb("gate", 2 * D), sb("merged", 2 * D), sb("sz", 1024), sb("tmp", 1024)
        r_t, ld = gate[:, 0:1024], gate[:, 1024:2048]
        iclr, cum, en = merged[:, 0:1024], merged[:, 1024:2048], sz
        lnp = gate
        k_t, b_t, v_t, ar = sb("k_t", 1024), sb("b_t", 1024), sb("v_t", 1024), sb("ar", 2048)
        vtok, lora, scm = sb("vtok", 1024), sb("lora", SEQ), sb("scm", 4096)
        T, TT, Wb, LM = sb("T", 1024), sb("TT", 1024), sb("Wb", 1024), sb("LM", 1024)
        btok, ktok, yt = T, LM, Wb
        lb, X, XT, subt = tmp[:, 0:256], tmp[:, 256:512], tmp[:, 512:768], tmp[:, 768:1024]
        up, bor = sb("up", W5), sb("bor", W5)
        q_tr, k_tr, v_a = sb("q_tr", 1024), sb("k_tr", 1024), sb("v_a", 1024)
        v_c, roped, rswap, kdup = sb("v_c", 256), sb("roped", 1024), sb("rswap", 512), sb("kdup", 512)
        prob, pT, otok = sb("prob", 1024), sb("pT", 1024), sb("otok", 512)
        S = [None, q_tr[:, 0:512], q_tr[:, 512:1024], k_tr[:, 0:512]]
        pch, uch, ysq = k_tr[:, 512:1024], v_a, pT
        cst, rot = sb("cst", C_ALL), sb("rot", 2 * 128)
        ang, turn = sb("ang", 128), sb("turn", 128)
        pos_i, pos_f = sb("pos_i", 2, i32), sb("pos_f", 2)
        id_bf, neg_bf = sb("id_bf", P, bf16), sb("neg_bf", 256, bf16)
        vrow, vcol = sb("vrow", P, rows=NVEC), sb("vcol", NVEC)
        omu, halves, sink, nsink = sb("omu", 17), sb("halves", 12), sb("sink", H), sb("nsink", H)
        mx, nb, den, rec, esk = sb("mx", 8), sb("nb", 8), sb("den", 8), sb("rec", 8), sb("esk", 8)
        ss, rn, mhalf, ec = sb("ss", 16), sb("rn", 16), sb("mhalf", 16), sb("ec", 16)
        rnt = sb("rnt", SEQ, rows=8)
        stat, agg, rstd = sb("stat", 24), sb("agg", 4), sb("rstd", 2)

        pb = [ctx.enter_context(nc.psum_tensor(f"pb{i}", [P, W5], f32)) for i in range(4)]
        wb = [ctx.enter_context(nc.psum_tensor(f"wb{i}", [P, W5], f32)) for i in range(4)]

        def sem(name):
            return ctx.enter_context(nc.semaphore(name))

        pe_done, act_done, dve_done, pool_done = sem("pe_done"), sem("act_done"), sem("dve_done"), sem("pool_done")
        done = dict(act=act_done, dve=dve_done)
        dve_chain, pool_chain = sem("dve_chain"), sem("pool_chain")
        cst_in, x_in, pos_in, vec_in, up_in, sink_in, ln_in = (sem(n) for n in ("cst_in", "x_in", "pos_in", "vec_in", "up_in", "sink_in", "ln_in"))
        x_out, lb_out, lb_in, t_out, t_in = (sem(n) for n in ("x_out", "lb_out", "lb_in", "t_out", "t_in"))
        raw_in = [sem(f"raw_in{i}") for i in range(RAW)]
        bf_ready, angles_ready, rot_ready, pos_ready = sem("bf_ready"), sem("angles_ready"), sem("rot_ready"), sem("pos_ready")

        ident, bones, centre = cst[:, C_ID:C_ID + P], cst[:, C_BO:C_BO + P], cst[:, C_CEN:C_CEN + P]
        MU, W0, A0, KK_, KA, RK_, GG, GB = 0, 17, 21, 25, 29, 33, 37, 41
        MUROW = {"lora": 12, "r": 0, "k": 4, "v": 8, "zB": 13}
        TDST = {"lora": lora, "r": r_t, "k": k_t, "v": v_t, "zB": k_t}

        def vec(row, j):
            return vcol[:, row + j:row + j + 1]

        def jt(buf, j, t=None):
            return buf[:, j * SEQ:(j + 1) * SEQ] if t is None else buf[:, j * SEQ + t * P:j * SEQ + (t + 1) * P]

        def cut(buf, t):
            return buf.rearrange("p (j t c) -> p j t c", t=2, c=P)[:, :, t, :]

        def col4(b, n=4):
            return b[:, 0:n * P].rearrange("p (j c) -> p j c", j=n)

        def slot(n):
            return slice((n % SPL) * 1024, (n % SPL) * 1024 + TILES[n][2] * UNITS[TILES[n][0]][4])

        def rslot(n):
            return slice((n % RAW) * 1024, (n % RAW) * 1024 + TILES[n][2] * UNITS[TILES[n][0]][4])

        def wbank(*w):
            return wb[WIDX[w] % 4]

        def pbank(unit, t):
            return pb[(UIDX[unit] % 2) * 2 + t]

        def z_part(x_, t):
            return k_t[:, t * 512:(t + 1) * 512] if x_ == "B" else pbank("z" + x_, t)[:, :]

        def heads_of(g):
            return (0, [g + 2 * i for i in range(4)]) if g < 2 else (1, [(g - 2) % 2 + 4 * ((g - 2) // 2) + 2 * i for i in range(2)])

        def rows(c):
            return slice(64 * (c % 2), 64 * (c % 2) + 64)

        def sco(h, t, part):
            o = ((t * 2 + h % 2) * 4 + h // 2) * 256 + 64 * part
            return slice(o, o + 64)

        def inv(h, t):
            o = (t * 8 + (h % 2) * 4 + h // 2) * CH
            return slice(o, o + CH)

        def counter(l):
            def at(eng, *m, back=False):
                return (l - 1 if back else l) * PER[eng] + NUM[eng][m]
            return at

        def linker(name, l):
            n = [0]

            def link():
                n[0] += 1
                return l * LINKS[name] + n[0]
            return link, n

        block = ctx.enter_context(nc.Block())

        @block.sync
        def _(sp):
            sp.dma_start(cst[:, :], consts).then_inc(cst_in, 16)
            for t in range(2):
                sp.dma_start(xres[:, t * D:(t + 1) * D], x[0, t * P:(t + 1) * P, :]).then_inc(x_in, 16)
            for t in range(2):
                sp.dma_start(pos_i[:, t:t + 1], positions[0, t * P:(t + 1) * P].unsqueeze(1)).then_inc(pos_in, 16)
            for l in range(DEPTH):
                at = counter(l)
                ly = slice(l, l + 1)
                if l:
                    sp.wait_ge(act_done, at("act", "exp", "C", 5, back=True))
                if l:
                    sp.wait_ge(dve_done, at("dve", "max", "C", 5, back=True))
                if l:
                    sp.wait_ge(dve_done, at("dve", "gn", back=True))
                sp.dma_start(vrow[0:17, :], mu_rwkv[ly, :].rearrange("a (r c) -> (a r) c", c=P)).then_inc(vec_in, 16)
                for i, v in ((0, w0), (1, a0), (2, k_k), (3, k_a), (5, gn_g), (6, gn_b)):
                    sp.dma_start(vrow[17 + 4 * i:21 + 4 * i, :], v[ly, :].rearrange("a (r c) -> (a r) c", c=P)).then_inc(vec_in, 16)
                sp.dma_start(vrow[33:37, :], r_k[ly, :, :].rearrange("a (r two) c -> (a r) (two c)", two=2)).then_inc(vec_in, 16)
                sp.dma_start(up[0:64, :], w_up[ly, :, :].rearrange("a p n -> (a p) n")).then_inc(up_in, 16)
                sp.dma_start(up[64:128, :], a_up[ly, :, :].rearrange("a p n -> (a p) n")).then_inc(up_in, 16)
                sp.dma_start(sink[:, :], sinks[ly, :].rearrange("a h -> (a h)").partition_broadcast(P)).then_inc(sink_in, 16)
                for n, (u, k0, kn) in enumerate(TILES):
                    _, _, src, c0, width, _ = UNITS[u]
                    if n == 38:
                        sp.wait_ge(dve_done, at("dve", "rs", 1, 1, 1))
                        for blk in range(8):
                            r0, c16 = 16 * blk, 16 * (blk % 4)
                            sp.dma_start(blocks[blk * 16:blk * 16 + 16, :].rearrange("n (s c) -> s n c", c=16),
                                         scm[r0:r0 + 16, :].rearrange("p (n c) -> p n c", c=256)[:, :, c16:c16 + 16]).then_inc(lb_out, 16)
                    if n == 39:
                        sp.wait_ge(lb_out, l * 128 + 128)
                        sp.dma_start(lb, blocks[:, :]).then_inc(lb_in, 16)
                    if n == 45:
                        sp.wait_ge(dve_done, at("dve", "sub", 2))
                        sp.dma_start(inverses[:, :], tmp[:, 256:768]).then_inc(t_out, 16)
                    if n == 46:
                        sp.wait_ge(t_out, l * 16 + 16)
                        sp.wait_ge(pool_done, at("pool", "zero"))
                        for i, dst in enumerate((T, TT)):
                            for blk in range(8):
                                r0, c16 = 16 * blk, 16 * (blk % 4)
                                sp.dma_start(dst[r0:r0 + 16, :].rearrange("p (n c) -> p n c", c=CH)[:, :, c16:c16 + 16],
                                             inverses[blk * 16:blk * 16 + 16, i * 256:(i + 1) * 256].rearrange("n (t c) -> t n c", c=16))\
                                    .then_inc(t_in, 16)
                    if l or not n < RAW:
                        sp.wait_ge(act_done, at("act", "hi", (n - RAW) % NT, back=n < RAW))
                    if l or not n < RAW:
                        sp.wait_ge(dve_done, at("dve", "lo", (n - RAW) % NT, back=n < RAW))
                    sp.dma_start(raw[:, rslot(n)].rearrange("p (k c) -> p k c", c=width),
                                 weights[src][ly, k0 * P:(k0 + kn) * P, c0:c0 + width]
                                 .rearrange("a (k p) c -> p (a k) c", p=P)).then_inc(raw_in[n % RAW], 16)
                sp.wait_ge(dve_done, at("dve", "bmul", "bB1"))
                sp.dma_start(lnp[:, 0:D], ln_g[ly, :].rearrange("a h -> (a h)").partition_broadcast(P)).then_inc(ln_in, 16)
                sp.dma_start(lnp[:, D:2 * D], ln_b[ly, :].rearrange("a h -> (a h)").partition_broadcast(P)).then_inc(ln_in, 16)
            for t in range(2):
                sp.wait_ge(dve_done, (DEPTH - 1) * PER["dve"] + NUM["dve"][("norm", t)])
                sp.dma_start(out[0, t * P:(t + 1) * P, :], xres[:, t * D:(t + 1) * D]).then_inc(x_out, 16)
            sp.wait_ge(x_out, 32)

        @block.tensor
        def _(pe):
            mm, tr = nc.tensor.matmul, nc.tensor.transpose
            pe.wait_ge(cst_in, 16)
            pe.wait_ge(bf_ready, 2)
            pe.wait_ge(x_in, 32)
            for l in range(DEPTH):
                at = counter(l)

                def fill(w):
                    i, kind, a = WIDX[w], w[0], w[1:]
                    b = wb[i % 4]
                    if i < 4:
                        last_user = [v for v in WORK if WIDX[v[1:]] % 4 == i][-1]
                        e, m = release(last_user[1:])
                        if l:
                            pe.wait_ge(done[e], at(e, *m, back=True))
                    else:
                        e, m = release(WORK[i - 4][1:])
                        pe.wait_ge(done[e], at(e, *m))
                    if kind == "xt":
                        t, h = a
                        if l:
                            pe.wait_ge(dve_done, at("dve", "norm", t, back=True))
                        for q in range(4):
                            last = tr(b[:, q * P:(q + 1) * P], xres[:, t * D + (4 * h + q) * P:t * D + (4 * h + q + 1) * P], ident)
                    elif kind == "vec":
                        pe.wait_ge(vec_in, l * 128 + 128)
                        last = tr(b[:, 0:NVEC], vrow[:, :], cst[0:NVEC, C_ID:C_ID + NVEC])
                    elif kind in ("dec", "icl"):
                        p0 = 0 if kind == "dec" else 64
                        pe.wait_ge(up_in, l * 32 + 32)
                        pe.wait_ge(act_done, at("act", "ltanh"))
                        for q in range(2):
                            last = mm(b[:, q * SEQ:(q + 1) * SEQ], up[p0:p0 + 64, (2 * a[0] + q) * P:(2 * a[0] + q + 1) * P],
                                      lora[p0:p0 + 64, :], start=True, stop=True)
                    elif kind == "nss":
                        src = b_t if a[0] == "k" else ysq
                        pe.wait_ge(act_done, at("act", *(("ksq",) if a[0] == "k" else ("cen", 1))))
                        for t in range(2):
                            for j in range(4):
                                last = mm(b[:, t * 8 + 2 * j:t * 8 + 2 * j + 2], jt(src, j, t), cst[:, C_SEL2:C_SEL2 + 2], start=True, stop=True)
                    elif kind == "nrt":
                        pe.wait_ge(pool_done, at("pool", "rn" + a[0]))
                        for t in range(2):
                            last = tr(b[0:8, t * P:(t + 1) * P], rn[:, t * 8:(t + 1) * 8], ident)
                    elif kind == "nrb":
                        pe.wait_ge(act_done, at("act", "nrt", a[0]))
                        for q in range(2):
                            j = 2 * a[1] + q
                            last = mm(b[:, q * SEQ:(q + 1) * SEQ], cst[0:8, C_SEL8 + j * P:C_SEL8 + (j + 1) * P], rnt[:, :],
                                      start=True, stop=True)
                    elif kind == "vt":
                        pe.wait_ge(dve_done, at("dve", "shift", "v"))
                        for j in range(4):
                            last = tr(b[:, j * P:(j + 1) * P], jt(v_t, j, a[0]), ident)
                    elif kind == "bt":
                        for j in range(4):
                            last = tr(b[:, j * P:(j + 1) * P], jt(b_t if a[0] == "b" else k_t, j, a[1]), ident)
                    elif kind == "bon":
                        pe.wait_ge(pool_done, at("pool", "rk"))
                        for q in range(2):
                            j = 2 * a[0] + q
                            last = mm(b[:, q * SEQ:(q + 1) * SEQ], bor[:, j * P:(j + 1) * P], jt(tmp, j), start=True, stop=True)
                    elif kind == "qt":
                        t = a[1]
                        if a[0] == "Ck":
                            pe.wait_ge(dve_done, at("dve", "ropek", t))
                            for n2 in range(2):
                                last = tr(b[:, n2 * P:(n2 + 1) * P], kdup[:, t * 256 + n2 * P:t * 256 + (n2 + 1) * P], ident)
                        else:
                            pe.wait_ge(dve_done, at("dve", "rope", a[0], t))
                            for j in range(4):
                                last = tr(b[:, j * P:(j + 1) * P], roped[:, t * W5 + j * P:t * W5 + (j + 1) * P], ident)
                    elif kind == "sc":
                        t, hs = heads_of(a[1])
                        keys = P * (t + 1)
                        pe.wait_ge(act_done, at("act", "qt", a[0] + "k", 1))
                        for i2, h in enumerate(hs):
                            p0, j = 64 * (h % 2), h // 2
                            kj = j if a[0] == "A" else h // 4
                            mm(b[:, i2 * keys:(i2 + 1) * keys], q_tr[p0:p0 + 64, j * SEQ + t * P:j * SEQ + (t + 1) * P],
                               k_tr[p0:p0 + 64, kj * SEQ:kj * SEQ + keys], start=(i2 == 0), stop=False, skip_group_check=True)
                        for i2, h in enumerate(hs):
                            if t == 1 and a[0] == "C":
                                mm(b[:, i2 * keys:i2 * keys + P], id_bf[:, :], neg_bf[:, P:2 * P], start=False, stop=False, skip_group_check=True)
                            last = mm(b[:, (i2 + 1) * keys - P:(i2 + 1) * keys], id_bf[:, :], neg_bf[:, 0:P], start=False,
                                      stop=(i2 == len(hs) - 1), skip_group_check=True)
                    elif kind == "pt":
                        pe.wait_ge(act_done, at("act", "exp", *a))
                        for q in range(4):
                            o = (a[1] % 2) * 512 + q * P
                            last = tr(b[:, q * P:(q + 1) * P], prob[:, o:o + P], ident)
                    elif kind == "pv":
                        t, hs = heads_of(a[1])
                        pe.wait_ge(act_done, at("act", "pt", *a))
                        pe.wait_ge(act_done, at("act", *(("Av",) if a[0] == "A" else ("vc",))))
                        for i2, h in enumerate(hs):
                            for kb in range(t + 1):
                                o = (a[1] % 2) * 512 + (i2 * (t + 1) + kb) * P
                                v = v_a[:, kb * W5 + h * HD:kb * W5 + (h + 1) * HD] if a[0] == "A" else \
                                    v_c[:, kb * P + (h // 4) * HD:kb * P + (h // 4 + 1) * HD]
                                last = mm(b[:, i2 * HD:(i2 + 1) * HD], pT[:, o:o + P], v, start=(kb == 0), stop=(kb == t))
                    elif kind == "ot":
                        pe.wait_ge(dve_done, at("dve", "pv", a[0], 1 if a[1] == 0 else 5))
                        for j in range(4):
                            last = tr(b[:, j * P:(j + 1) * P], otok[:, j * P:(j + 1) * P], ident)
                    elif kind == "rs":
                        t, par, half = a
                        pe.wait_ge(pool_done, at("pool", "kt"))
                        pe.wait_ge(dve_done, at("dve", "kb"))
                        p0 = 64 * par
                        for i2 in range(2):
                            j = 2 * half + i2
                            for c in (2 * t, 2 * t + 1):
                                for q, src in enumerate((b_t, k_t)):
                                    last = mm(b[rows(c), i2 * 256 + q * 128:i2 * 256 + (q + 1) * 128],
                                              src[p0:p0 + 64, j * SEQ + c * CH:j * SEQ + (c + 1) * CH],
                                              ar[p0:p0 + 64, (j * NC + c) * 128:(j * NC + c + 1) * 128], start=True, stop=True)
                    elif kind in ("w1", "w2", "t1", "tt1", "tt2"):
                        cp, t = a
                        r = rows(cp)
                        lhs, rhs = {"w": (LM, T), "t": (TT, Wb), "tt": (Wb, TT)}[kind[:-1]]
                        if kind == "w1":
                            pe.wait_ge(t_in, l * 256 + 256)
                            pe.wait_ge(pool_done, at("pool", "lm1"))
                        elif kind == "w2":
                            pe.wait_ge(pool_done, at("pool", "lm2"))
                            pe.wait_ge(dve_done, at("dve", "t1", 1, 1))
                        elif kind == "tt2":
                            pe.wait_ge(act_done, at("act", "w2", 1, 1))
                            pe.wait_ge(dve_done, at("dve", "tt1", 1, 1))
                        else:
                            pe.wait_ge(act_done, at("act", "w1", 1, 1))
                        for h in range(8):
                            o = slice((t * 8 + h) * CH, (t * 8 + h + 1) * CH)
                            last = mm(b[r, h * CH:(h + 1) * CH], lhs[r, o], rhs[r, o], start=True, stop=True)
                    elif kind == "cp":
                        c, t, r = a[0], a[0] // 2, rows(a[0])
                        pe.wait_ge(act_done, at("act", "vt", 1))
                        if c > 0:
                            pe.wait_ge(dve_done, at("dve", "cs", c - 1))
                            for j in range(4):
                                mm(b[r, j * P:(j + 1) * P], ar[:, (j * NC + c) * 128:(j * NC + c) * 128 + 64],
                                   S[c][:, j * P:(j + 1) * P], start=(j == 0), stop=False, skip_group_check=True)
                        for h in range(8):
                            last = mm(b[r, h * HD:(h + 1) * HD], scm[r, sco(h, t, 2)], vtok[r, t * W5 + h * HD:t * W5 + (h + 1) * HD],
                                      start=(c == 0 and h == 0), stop=(h == 7), skip_group_check=True)
                    elif kind == "cu":
                        c, t, r = a[0], a[0] // 2, rows(a[0])
                        pe.wait_ge(act_done, at("act", "cp", c))
                        pe.wait_ge(dve_done, at("dve", "tt2", 1, 1))
                        for h in range(8):
                            last = mm(b[r, h * HD:(h + 1) * HD], TT[r, inv(h, t)], pch[r, h * HD:(h + 1) * HD], start=True, stop=True)
                    elif kind == "cs":
                        c, t, r = a[0], a[0] // 2, rows(a[0])
                        pe.wait_ge(dve_done, at("dve", "cu", c))
                        pe.wait_ge(act_done, at("act", "bt", "k", 1))
                        for j in range(4):
                            o = slice(t * W5 + j * P, t * W5 + (j + 1) * P)
                            mm(b[:, j * P:(j + 1) * P], btok[r, o], uch[r, o], start=True, stop=False)
                            last = mm(b[:, j * P:(j + 1) * P], ktok[r, o], vtok[r, o], start=False, stop=True)
                    elif kind == "cy":
                        c, t, r = a[0], a[0] // 2, rows(a[0])
                        pe.wait_ge(dve_done, at("dve", "cu", c))
                        if c > 0:
                            for j in range(4):
                                mm(b[:, j * CH:(j + 1) * CH], S[c][:, j * P:(j + 1) * P],
                                   ar[:, (j * NC + c) * 128 + 64:(j * NC + c + 1) * 128], start=(j == 0), stop=False, skip_group_check=True)
                        for h in range(8):
                            vc = slice(t * W5 + h * HD, t * W5 + (h + 1) * HD)
                            o = b[64 * (h % 2):64 * (h % 2) + 64, (h // 2) * CH:(h // 2 + 1) * CH]
                            mm(o, uch[r, vc], scm[r, sco(h, t, 1)], start=(c == 0 and h < 2), stop=False, skip_group_check=True)
                            last = mm(o, vtok[r, vc], scm[r, sco(h, t, 3)], start=False, stop=(h >= 6), skip_group_check=True)
                    elif kind == "cen":
                        pe.wait_ge(act_done, at("act", "cy", NC - 1))
                        last = mm(b[:, :], centre, yt[:, a[0] * 512:(a[0] + 1) * 512], start=True, stop=True)
                    elif kind == "mt":
                        t, h = a
                        pe.wait_ge(pool_done, at("pool", "addB1"))
                        for q in range(4):
                            last = tr(b[:, q * P:(q + 1) * P], merged[:, t * D + (4 * h + q) * P:t * D + (4 * h + q + 1) * P], ident)
                    last.then_inc(pe_done, 1)

                def project(n):
                    u, k0, kn = TILES[n]
                    name, lay, _, _, width, _ = UNITS[u]
                    first, final = k0 == 0, n == LAST[u]
                    pe.wait_ge(act_done, at("act", "hi", n))
                    pe.wait_ge(dve_done, at("dve", "lo", n))
                    if first:
                        e, m = unit_release(UNITS[(u - 2) % len(UNITS)][0])
                        if l or not u < 2:
                            pe.wait_ge(done[e], at(e, *m, back=u < 2))
                        if name == "lora":
                            pe.wait_ge(act_done, at("act", "xth", 1, 1))
                            pe.wait_ge(dve_done, at("dve", "xtl", 1, 1))
                        elif name == "o0":
                            pe.wait_ge(act_done, at("act", "mth", 1, 1))
                            pe.wait_ge(dve_done, at("dve", "mtl", 1, 1))
                        elif name[0] == "b":
                            pe.wait_ge(act_done, at("act", "ghi", name[1]))
                            pe.wait_ge(dve_done, at("dve", "glo", name[1]))
                    ahi, alo = (g_hi, g_lo) if name[0] == "b" else (xt_hi, xt_lo)
                    hi, lo = w_hi[:, slot(n)], w_lo[:, slot(n)]
                    if lay == "T":
                        for kk in range(kn):
                            ah, al = jt(ahi, k0 + kk), jt(alo, k0 + kk)
                            for j in range(width // P):
                                o = pbank(name, j // 2)[:, (j % 2) * SEQ:(j % 2 + 1) * SEQ]
                                cs = slice(kk * width + j * P, kk * width + (j + 1) * P)
                                mm(o, hi[:, cs], ah, start=(first and kk == 0 and j % 2 == 0), stop=False, skip_group_check=True)
                                mm(o, hi[:, cs], al, start=False, stop=False, skip_group_check=True)
                                last = mm(o, lo[:, cs], ah, start=False, stop=(final and kk == kn - 1), skip_group_check=True)
                    else:
                        for t in range(2):
                            o = pbank(name, t)[:, 0:width]
                            for kk in range(kn):
                                cs = slice(kk * width, (kk + 1) * width)
                                ah, al = jt(ahi, k0 + kk, t), jt(alo, k0 + kk, t)
                                mm(o, ah, hi[:, cs], start=(first and kk == 0), stop=False)
                                mm(o, ah, lo[:, cs], start=False, stop=False)
                                last = mm(o, al, hi[:, cs], start=False, stop=(final and kk == kn - 1))
                    last.then_inc(pe_done, 1)

                for _, *m in PE_ORDER:
                    if m[0] == "tile":
                        project(m[1])
                    else:
                        fill(tuple(m))

        @block.scalar
        def _(act):
            A = nc.scalar.activation
            act.wait_ge(cst_in, 16)
            A(id_bf[:, :], ident, ACT.Copy).then_inc(bf_ready, 1)
            A(neg_bf[:, :], cst[:, C_NEG:C_NEG + 256], ACT.Copy).then_inc(bf_ready, 1)
            act.wait_ge(angles_ready, 1)
            for t in range(2):
                r = rot[:, t * 128:(t + 1) * 128].rearrange("p (f two d) -> p f two d", f=2, two=2)
                sn, cs = ang[:, t * 32:(t + 1) * 32], ang[:, 64 + t * 32:64 + (t + 1) * 32]
                A(r[:, 0, 0, :], cs, ACT.Sin)
                A(r[:, 0, 1, :], cs, ACT.Sin)
                A(r[:, 1, 0, :], sn, ACT.Sin, scale=-1.0)
                last = A(r[:, 1, 1, :], sn, ACT.Sin)
            last.then_inc(rot_ready, 1)
            for l in range(DEPTH):
                at = counter(l)

                def run(kind, *a):
                    m = (kind,) + a
                    if m in WIDX:
                        act.wait_ge(pe_done, at("pe", *m))
                        b = wbank(*m)
                    if kind == "hi":
                        n = a[0]
                        act.wait_ge(raw_in[n % RAW], l * (16 * NT // RAW) + 16 * (n // RAW + 1))
                        if l or not n < SPL:
                            act.wait_ge(pe_done, at("pe", "tile", (n - SPL) % NT, back=n < SPL))
                        return A(w_hi[:, slot(n)], raw[:, rslot(n)], ACT.Copy).then_inc(act_done, 1)
                    if kind in ("xth", "mth"):
                        src = {"xth": "xt", "mth": "mt"}[kind]
                        act.wait_ge(pe_done, at("pe", src, *a))
                        return A(cut(xt_hi[:, :], a[0])[:, 4 * a[1]:4 * a[1] + 4, :], col4(wbank(src, *a)), ACT.Copy,
                                 scale=1.0 if kind == "xth" else 0.5).then_inc(act_done, 1)
                    if kind == "vec":
                        return A(vcol[:, :], b[:, 0:NVEC], ACT.Copy).then_inc(act_done, 1)
                    if kind == "mix":
                        name = a[0]
                        act.wait_ge(pe_done, at("pe", "tile", LAST[UIDX[name]]))
                        act.wait_ge(dve_done, at("dve", "derive"))
                        if name == "zB":
                            act.wait_ge(pe_done, at("pe", "bt", "k", 1))
                        for j in range(UNITS[UIDX[name]][4] // P):
                            last = A(jt(TDST[name], j), pbank(name, j // 2)[:, (j % 2) * SEQ:(j % 2 + 1) * SEQ], ACT.Copy,
                                     scale=omu[:, MUROW[name] + j:MUROW[name] + j + 1])
                        return last.then_inc(act_done, 1)
                    if kind == "ltanh":
                        act.wait_ge(dve_done, at("dve", "shift", "lora"))
                        return A(lora[0:64, :], lora[0:64, :], ACT.Tanh).then_inc(act_done, 1)
                    if kind in ("dec", "icl"):
                        dst, hc = (ld, 0) if kind == "dec" else (iclr, 4)
                        for q in range(2):
                            j = 2 * a[0] + q
                            last = A(jt(dst, j), b[:, q * SEQ:(q + 1) * SEQ], ACT.Tanh, scale=0.5, bias=halves[:, hc + j:hc + j + 1])
                        return last.then_inc(act_done, 1)
                    if kind == "en":
                        act.wait_ge(dve_done, at("dve", "scan"))
                        return A(en[:, :], cum, ACT.Exp, scale=-1.0).then_inc(act_done, 1)
                    if kind == "ex":
                        act.wait_ge(pool_done, at("pool", "cx"))
                        return A(ld, ld, ACT.Exp).then_inc(act_done, 1)
                    if kind == "ei":
                        return A(cum, cum, ACT.Exp).then_inc(act_done, 1)
                    if kind == "ec":
                        act.wait_ge(act_done, at("act", "ei"))
                        return A(ec[:, :], cum.rearrange("p (c t) -> p c t", t=CH)[:, :, CH - 1], ACT.Copy).then_inc(act_done, 1)
                    if kind == "ksq":
                        act.wait_ge(dve_done, at("dve", "shift", "k"))
                        for j in range(4):
                            last = A(jt(b_t, j), jt(k_t, j), ACT.Square, scale=vec(KK_, j))
                        return last.then_inc(act_done, 1)
                    if kind == "nrt":
                        return A(rnt[:, :], b[0:8, 0:SEQ], ACT.Copy).then_inc(act_done, 1)
                    if kind == "vt":
                        return A(vtok[:, a[0] * W5:(a[0] + 1) * W5], b[:, :], ACT.Copy).then_inc(act_done, 1)
                    if kind == "bt":
                        act.wait_ge(dve_done, at("dve", "tt2", 1, 1))
                        return A((btok if a[0] == "b" else ktok)[:, a[1] * W5:(a[1] + 1) * W5], b[:, :], ACT.Copy).then_inc(act_done, 1)
                    if kind == "qt":
                        dst, n = (q_tr, 4) if a[0][1] == "q" else (k_tr, 2 if a[0] == "Ck" else 4)
                        return A(cut(dst[:, 0:n * SEQ], a[1]), col4(b, n), ACT.Copy).then_inc(act_done, 1)
                    if kind == "exp":
                        x_, g = a
                        t, hs = heads_of(g)
                        keys, o4 = P * (t + 1), (g % 2) * 4
                        act.wait_ge(dve_done, at("dve", "max", x_, g))
                        if x_ == "C":
                            A(esk[:, o4:o4 + len(hs)], esk[:, o4:o4 + len(hs)], ACT.Exp)
                        for i2, h in enumerate(hs):
                            o = (g % 2) * 512 + i2 * keys
                            last = A(prob[:, o:o + keys], wbank("sc", *a)[:, i2 * keys:(i2 + 1) * keys], ACT.Exp, scale=SCALE,
                                     bias=nb[:, o4 + i2:o4 + i2 + 1], accum_out=den[:, o4 + i2:o4 + i2 + 1])
                        return last.then_inc(act_done, 1)
                    if kind == "pt":
                        x_, g = a
                        if g >= 2:
                            act.wait_ge(dve_done, at("dve", "pv", x_, g - 2))
                        elif x_ == "C":
                            act.wait_ge(dve_done, at("dve", "pv", "A", g + 4))
                        return A(pT[:, (g % 2) * 512:(g % 2) * 512 + 512], b[:, :], ACT.Copy).then_inc(act_done, 1)
                    if kind == "ot":
                        return A(cut({"A": o_A, "C": o_C}[a[0]][:, :], a[1]), col4(b), ACT.Copy).then_inc(act_done, 1)
                    if kind in ("w1", "w2"):
                        if kind == "w2":
                            act.wait_ge(dve_done, at("dve", "tt1", 1, 1))
                        r = rows(a[0])
                        return A(Wb[r, a[1] * 512:(a[1] + 1) * 512], b[r, :], ACT.Copy).then_inc(act_done, 1)
                    if kind == "cp":
                        return A(pch[rows(a[0]), :], b[rows(a[0]), :], ACT.Copy).then_inc(act_done, 1)
                    if kind == "cy":
                        dst = yt[:, :].rearrange("p (j c) -> p j c", j=4)[:, :, a[0] * CH:(a[0] + 1) * CH]
                        return A(dst, b[:, 0:256].rearrange("p (j c) -> p j c", j=4), ACT.Copy).then_inc(act_done, 1)
                    if kind == "cen":
                        A(b_t[:, a[0] * 512:(a[0] + 1) * 512], b[:, :], ACT.Copy)
                        return A(ysq[:, a[0] * 512:(a[0] + 1) * 512], b[:, :], ACT.Square).then_inc(act_done, 1)
                    if kind in ("Av", "vc"):
                        name = {"Av": "Av", "vc": "Ckv"}[kind]
                        act.wait_ge(pe_done, at("pe", "tile", LAST[UIDX[name]]))
                        dst, w = (v_a, W5) if kind == "Av" else (v_c, P)
                        for t in range(2):
                            src = pbank(name, t)[:, :] if kind == "Av" else pbank(name, t)[:, P:2 * P]
                            last = A(dst[:, t * w:(t + 1) * w], src, ACT.Copy)
                        return last.then_inc(act_done, 1)
                    if kind == "ztanh":
                        name = "z" + a[0]
                        act.wait_ge(pe_done, at("pe", "tile", LAST[UIDX[name]]))
                        if a[0] == "A":
                            act.wait_ge(dve_done, at("dve", "kb"))
                            act.wait_ge(pool_done, at("pool", "kt"))
                        else:
                            act.wait_ge(dve_done, at("dve", "glo", {"C": "A", "B": "C"}[a[0]]))
                        if a[0] == "B":
                            act.wait_ge(dve_done, at("dve", "shift", "zB"))
                        for t in range(2):
                            last = A(sz[:, t * 512:(t + 1) * 512], z_part(a[0], t), ACT.Tanh, scale=0.5)
                        return last.then_inc(act_done, 1)
                    if kind == "gate":
                        name, c = a[0], int(a[0][2])
                        act.wait_ge(pe_done, at("pe", "tile", LAST[UIDX[name]]))
                        if name[1] == "A":
                            act.wait_ge(dve_done, at("dve", "rs", 1, 1, 1))
                        else:
                            act.wait_ge(dve_done, at("dve", "bmul", "b" + {"C": "A", "B": "C"}[name[1]] + name[2]))
                        for t in range(2):
                            last = A(gate[:, t * D + c * 512:t * D + (c + 1) * 512], pbank(name, t)[:, :], ACT.Tanh, scale=0.5)
                        return last.then_inc(act_done, 1)
                    if kind == "ghi":
                        act.wait_ge(dve_done, at("dve", "g", a[0]))
                        if a[0] != "A":
                            act.wait_ge(pe_done, at("pe", "tile", LAST[UIDX["b" + {"C": "A", "B": "C"}[a[0]] + "1"]]))
                        return A(g_hi[:, :], sz[:, :], ACT.Copy).then_inc(act_done, 1)
                    raise ValueError(kind)

                for i, (_, *m) in enumerate(ACT_ORDER):
                    if i and m[0] != "hi":
                        act.wait_ge(act_done, at("act", *ACT_ORDER[i - 1][1:]))
                    run(*m)

        @block.vector
        def _(dve):
            tt, ts, stt = nc.vector.tensor_tensor, nc.vector.tensor_scalar, nc.vector.scalar_tensor_tensor
            pre = [0]

            def then(ins):
                pre[0] += 1
                ins.then_inc(pos_ready, 1)
                dve.wait_ge(pos_ready, pre[0])

            dve.wait_ge(cst_in, 16)
            dve.wait_ge(pos_in, 32)
            then(nc.vector.tensor_copy(pos_f[:, :], pos_i[:, :]))
            for f in range(2):
                for t in range(2):
                    o = ang[:, f * 64 + t * 32:f * 64 + (t + 1) * 32]
                    last = ts(o, cst[:, C_INV:C_INV + 32], pos_f[:, t:t + 1], None, ALU.mult)
            then(last)
            for f in range(2):
                last = ts(turn[:, f * 64:(f + 1) * 64], ang[:, f * 64:(f + 1) * 64], 1 / (2 * math.pi), 0.25 * f, ALU.mult, ALU.add)
            then(last)
            then(ts(turn[:, :], turn[:, :], ROUND, None, ALU.add))
            then(ts(turn[:, :], turn[:, :], ROUND, None, ALU.subtract))
            for c in TWO_PI:
                then(stt(ang[:, :], turn[:, :], -c, ang[:, :], ALU.mult, ALU.add))
            then(ts(ang[:, 64:128], ang[:, 64:128], math.pi / 2, None, ALU.add))
            ts(ang[:, :], ang[:, :], PI_MAX, -PI_MAX, ALU.min, ALU.max).then_inc(angles_ready, 1)
            nc.vector.memset(mhalf[:, :], -0.5)
            dve.wait_ge(rot_ready, 1)

            for l in range(DEPTH):
                at = counter(l)
                link, links = linker("dve", l)

                def run(kind, *a):
                    m = (kind,) + a
                    if m in WIDX:
                        dve.wait_ge(pe_done, at("pe", *m))
                        b = wbank(*m)
                    if kind == "lo":
                        n = a[0]
                        dve.wait_ge(act_done, at("act", "hi", n))
                        return tt(w_lo[:, slot(n)], raw[:, rslot(n)], w_hi[:, slot(n)].bitcast(f32), ALU.subtract).then_inc(dve_done, 1)
                    if kind == "xtl":
                        dve.wait_ge(act_done, at("act", "xth", *a))
                        half = lambda buf: cut(buf, a[0])[:, 4 * a[1]:4 * a[1] + 4, :]
                        return tt(half(xt_lo[:, :]), col4(wbank("xt", *a)), half(xt_hi[:, :].bitcast(f32)), ALU.subtract).then_inc(dve_done, 1)
                    if kind == "mtl":
                        dve.wait_ge(act_done, at("act", "mth", *a))
                        half = lambda buf: cut(buf, a[0])[:, 4 * a[1]:4 * a[1] + 4, :]
                        return stt(half(xt_lo[:, :]), col4(wbank("mt", *a)), 0.5, half(xt_hi[:, :].bitcast(f32)), ALU.mult, ALU.subtract).then_inc(dve_done, 1)
                    if kind == "derive":
                        dve.wait_ge(act_done, at("act", "vec"))
                        dve.wait_ge(sink_in, l * 16 + 16)
                        ts(omu[:, :], vcol[:, MU:MU + 17], -1.0, 1.0, ALU.mult, ALU.add)
                        ts(halves[:, 0:8], vcol[:, W0:W0 + 8], 0.5, None, ALU.mult)
                        ts(halves[:, 8:12], vcol[:, KA:KA + 4], 0.5, None, ALU.mult)
                        for j in range(4):
                            ts(bor[:, j * P:(j + 1) * P], bones, vec(RK_, j), None, ALU.mult)
                        return ts(nsink[:, :], sink[:, :], -1.0, None, ALU.mult).then_inc(dve_done, 1)
                    if kind == "shift":
                        name = a[0]
                        dve.wait_ge(act_done, at("act", "mix", name))
                        for j in range(UNITS[UIDX[name]][4] // P):
                            o = jt(TDST[name], j)[:, 1:SEQ]
                            h = pbank(name, j // 2)[:, (j % 2) * SEQ:(j % 2) * SEQ + SEQ - 1]
                            last = stt(o, h, vec(MUROW[name], j), o, ALU.mult, ALU.add)
                        return last.then_inc(dve_done, 1)
                    if kind == "ld":
                        dve.wait_ge(act_done, at("act", "dec", 1))
                        return ts(ld, ld, -DECAY_SCALE / 2, -DECAY_SCALE / 2, ALU.mult, ALU.add).then_inc(dve_done, 1)
                    if kind == "scan":
                        dve.wait_ge(dve_done, at("dve", "ld"))
                        for j in range(4):
                            last = nc.vector.tensor_tensor_scan(jt(cum, j), cst[:, C_RST:C_RST + SEQ], jt(ld, j), 0.0, ALU.mult, ALU.add)
                        return last.then_inc(dve_done, 1)
                    if kind == "ta":
                        dve.wait_ge(act_done, at("act", "icl", 1))
                        for j in range(4):
                            last = ts(jt(tmp, j), jt(iclr, j), 1.0, halves[:, 8 + j:9 + j], ALU.subtract, ALU.mult)
                        last.then_inc(dve_chain, 1)
                        dve.wait_ge(dve_chain, link())
                        return ts(iclr, iclr, 0.5, 0.5, ALU.mult, ALU.add).then_inc(dve_done, 1)
                    if kind == "nss":
                        if a[0] == "k":
                            return ts(ss[:, :], b[:, 0:16], 1e-24, None, ALU.max).then_inc(dve_done, 1)
                        return ts(ss[:, :], b[:, 0:16], 1.0 / HD, GN_EPS, ALU.mult, ALU.add).then_inc(dve_done, 1)
                    if kind == "nrb":
                        if a[0] == "k":
                            for q in range(2):
                                j = 2 * a[1] + q
                                last = stt(jt(b_t, j), jt(k_t, j), vec(KK_, j), b[:, q * SEQ:(q + 1) * SEQ], ALU.mult, ALU.mult)
                            return last.then_inc(dve_done, 1)
                        o = b_t[:, a[1] * 512:(a[1] + 1) * 512]
                        return tt(o, o, b[:, :], ALU.mult).then_inc(dve_done, 1)
                    if kind == "k2":
                        dve.wait_ge(dve_done, at("dve", "nrb", "k", 1))
                        return stt(k_t[:, :], tmp[:, :], 1.0, k_t[:, :], ALU.add, ALU.mult).then_inc(dve_done, 1)
                    if kind == "ara":
                        dve.wait_ge(act_done, at("act", "ex"))
                        o = ar[:, :].rearrange("p (n two t) -> p n two t", two=2, t=CH)[:, :, 0, :]
                        return stt(o, b_t[:, :].rearrange("p (n t) -> p n t", t=CH), -1.0, ld.rearrange("p (n t) -> p n t", t=CH),
                                   ALU.mult, ALU.mult).then_inc(dve_done, 1)
                    if kind == "kb":
                        tt(b_t[:, :], b_t[:, :], iclr, ALU.mult).then_inc(dve_chain, 1)
                        dve.wait_ge(dve_chain, link())
                        dve.wait_ge(act_done, at("act", "en"))
                        return tt(b_t[:, :], b_t[:, :], en[:, :], ALU.mult).then_inc(dve_done, 1)
                    if kind == "bon":
                        dve.wait_ge(act_done, at("act", "vt", 1))
                        o = v_t[:, a[0] * 512:(a[0] + 1) * 512]
                        return tt(o, o, b[:, :], ALU.mult).then_inc(dve_done, 1)
                    if kind in ("rope", "ropek"):
                        name, t = (a[0], a[1]) if kind == "rope" else ("Ckv", a[0])
                        n = H if kind == "rope" else 2
                        dve.wait_ge(pe_done, at("pe", "tile", LAST[UIDX[name]]))
                        if name == "Ak":
                            dve.wait_ge(act_done, at("act", "qt", "Aq", t))
                        elif name == "Cq":
                            dve.wait_ge(act_done, at("act", "qt", "Ak", t))
                        elif name == "Ckv":
                            dve.wait_ge(act_done, at("act", "vc"))
                        src = pbank(name, t)[:, 0:n * HD]
                        if kind == "rope":
                            o = roped[:, t * W5:(t + 1) * W5].rearrange("p (n d) -> p n d", d=HD)
                        else:
                            kd = kdup[:, t * 256:(t + 1) * 256].rearrange("p (n two d) -> p n two d", two=2, d=HD)
                            o = kd[:, :, 0, :]
                        cos2 = rot[:, t * 128:t * 128 + 64].unsqueeze(1).to_broadcast([P, n, HD])
                        sin2 = rot[:, t * 128 + 64:(t + 1) * 128].rearrange("p (two d) -> p two d", two=2).unsqueeze(1).to_broadcast([P, n, 2, 32])
                        sw = rswap[:, 0:n * HD].rearrange("p (n two d) -> p n two d", two=2, d=32)
                        tt(o, src.rearrange("p (n d) -> p n d", d=HD), cos2, ALU.mult)
                        tt(sw, src.rearrange("p (n two d) -> p n two d", two=2, d=32)[:, :, ::-1, :], sin2, ALU.mult).then_inc(dve_chain, 1)
                        dve.wait_ge(dve_chain, link())
                        last = tt(o, o, rswap[:, 0:n * HD].rearrange("p (n d) -> p n d", d=HD), ALU.add)
                        if kind == "ropek":
                            last.then_inc(dve_chain, 1)
                            dve.wait_ge(dve_chain, link())
                            last = nc.vector.tensor_copy(kd[:, :, 1, :], kd[:, :, 0, :])
                        return last.then_inc(dve_done, 1)
                    if kind == "max":
                        x_, g = a
                        t, hs = heads_of(g)
                        n, o4 = len(hs), (g % 2) * 4
                        dve.wait_ge(pe_done, at("pe", "sc", *a))
                        if g >= 2:
                            dve.wait_ge(act_done, at("act", "exp", x_, g - 2))
                        elif x_ == "C":
                            dve.wait_ge(act_done, at("act", "exp", "A", g + 4))
                        nc.vector.reduce_max(mx[:, o4:o4 + n], wbank("sc", *a)[:, :].rearrange("p (n k) -> p n k", n=n), AX.X).then_inc(dve_chain, 1)
                        dve.wait_ge(dve_chain, link())
                        if x_ == "A":
                            return ts(nb[:, o4:o4 + n], mx[:, o4:o4 + n], -SCALE, None, ALU.mult).then_inc(dve_done, 1)
                        if g >= 2:
                            dve.wait_ge(dve_done, at("dve", "pv", x_, g - 2))
                        sk = slice(hs[0], hs[-1] + 1, 2)
                        stt(nb[:, o4:o4 + n], mx[:, o4:o4 + n], -SCALE, nsink[:, sk], ALU.mult, ALU.min).then_inc(dve_chain, 1)
                        dve.wait_ge(dve_chain, link())
                        return tt(esk[:, o4:o4 + n], sink[:, sk], nb[:, o4:o4 + n], ALU.add).then_inc(dve_done, 1)
                    if kind == "pv":
                        x_, g = a
                        t, hs = heads_of(g)
                        n, o4 = len(hs), (g % 2) * 4
                        dve.wait_ge(act_done, at("act", "exp", x_, g))
                        if x_ == "C":
                            tt(den[:, o4:o4 + n], den[:, o4:o4 + n], esk[:, o4:o4 + n], ALU.add).then_inc(dve_chain, 1)
                            dve.wait_ge(dve_chain, link())
                        nc.vector.reciprocal(rec[:, o4:o4 + n], den[:, o4:o4 + n]).then_inc(dve_chain, 1)
                        dve.wait_ge(dve_chain, link())
                        if g >= 2:
                            dve.wait_ge(act_done, at("act", "ot", x_, 0))
                        elif x_ == "C":
                            dve.wait_ge(act_done, at("act", "ot", "A", 1))
                        o = otok[:, :].rearrange("p (q two d) -> p q two d", two=2, d=HD)[:, hs[0] // 2:hs[0] // 2 + n, hs[0] % 2, :]
                        return tt(o, b[:, 0:n * HD].rearrange("p (n d) -> p n d", d=HD),
                                  rec[:, o4:o4 + n].unsqueeze(2).to_broadcast([P, n, HD]), ALU.mult).then_inc(dve_done, 1)
                    if kind == "rs":
                        t, par, half = a
                        o = scm[:, ((t * 2 + par) * 4 + 2 * half) * 256:((t * 2 + par) * 4 + 2 * half + 2) * 256]
                        return tt(o.rearrange("p (n c) -> p n c", c=P), b[:, :].rearrange("p (n c) -> p n c", c=P),
                                  cst[:, C_MSK:C_MSK + P].unsqueeze(1).to_broadcast([P, 4, P]), ALU.mult).then_inc(dve_done, 1)
                    if kind == "sub":
                        if a[0] == 0:
                            dve.wait_ge(lb_in, l * 16 + 16)
                            nc.vector.tensor_copy(X, cst[:, C_EYE16:C_EYE16 + 256]).then_inc(dve_chain, 1)
                            dve.wait_ge(dve_chain, link())
                        else:
                            dve.wait_ge(dve_done, at("dve", "sub", a[0] - 1))
                        x3, l3 = X.rearrange("p (t c) -> p t c", c=16), lb.rearrange("p (s t) -> p s t", t=16)
                        for s in range(5 * a[0], 5 * a[0] + 5):
                            n, c = 15 - s, s + 1
                            pr = subt[:, 0:n * c].rearrange("p (t c) -> p t c", c=c)
                            tt(pr, l3[:, s, s + 1:16].unsqueeze(2).to_broadcast([P, n, c]),
                                    x3[:, s, 0:c].unsqueeze(1).to_broadcast([P, n, c]), ALU.mult).then_inc(dve_chain, 1)
                            dve.wait_ge(dve_chain, link())
                            last = tt(x3[:, s + 1:16, 0:c], x3[:, s + 1:16, 0:c], pr, ALU.add)
                            if s < 5 * a[0] + 4:
                                last.then_inc(dve_chain, 1)
                                dve.wait_ge(dve_chain, link())
                        if a[0] == 2:
                            last.then_inc(dve_chain, 1)
                            dve.wait_ge(dve_chain, link())
                            last = nc.vector.tensor_copy(XT.rearrange("p (c t) -> p c t", t=16), X.rearrange("p (t c) -> p c t", c=16))
                        return last.then_inc(dve_done, 1)
                    if kind in ("t1", "tt1", "tt2"):
                        dst = T if kind == "t1" else TT
                        o = dst[rows(a[0]), a[1] * 512:(a[1] + 1) * 512]
                        return tt(o, o, b[rows(a[0]), :], ALU.add).then_inc(dve_done, 1)
                    if kind == "cu":
                        c = a[0]
                        return nc.vector.tensor_copy(uch[rows(c), (c // 2) * W5:(c // 2 + 1) * W5], b[rows(c), :]).then_inc(dve_done, 1)
                    if kind == "cs":
                        c = a[0]
                        dve.wait_ge(pool_done, at("pool", "states"))
                        for p_ in range(2):
                            r = slice(64 * p_, 64 * p_ + 64)
                            blk = lambda buf: buf[r, :].rearrange("p (j two v) -> p j two v", two=2, v=HD)[:, :, p_, :]
                            e = ec[r, :].rearrange("p (j c) -> p j c", c=NC)[:, :, c].unsqueeze(2).to_broadcast([64, 4, HD])
                            if c == 0:
                                last = tt(blk(S[1]), blk(b), e, ALU.mult)
                            else:
                                tt(blk(S[c + 1]), blk(b), blk(S[c]), ALU.add).then_inc(dve_chain, 1)
                                dve.wait_ge(dve_chain, link())
                                last = tt(blk(S[c + 1]), blk(S[c + 1]), e, ALU.mult)
                        return last.then_inc(dve_done, 1)
                    if kind == "gn":
                        dve.wait_ge(dve_done, at("dve", "nrb", "y", 1))
                        for j in range(4):
                            last = ts(jt(b_t, j), jt(b_t, j), vec(GG, j), vec(GB, j), ALU.mult, ALU.add)
                        last.then_inc(dve_chain, 1)
                        dve.wait_ge(dve_chain, link())
                        return tt(v_t[:, :], v_t[:, :], b_t[:, :], ALU.add).then_inc(dve_done, 1)
                    if kind == "sz":
                        dve.wait_ge(act_done, at("act", "ztanh", a[0]))
                        for t in range(2):
                            o = sz[:, t * 512:(t + 1) * 512]
                            last = stt(o, o, 1.0, z_part(a[0], t), ALU.add, ALU.mult)
                        return last.then_inc(dve_done, 1)
                    if kind == "g":
                        dve.wait_ge(dve_done, at("dve", "sz", a[0]))
                        if a[0] == "B":
                            dve.wait_ge(dve_done, at("dve", "gn"))
                        else:
                            dve.wait_ge(act_done, at("act", "ot", a[0], 1))
                        return stt(sz[:, :], {"A": o_A, "C": o_C, "B": v_t}[a[0]][:, :], 0.5, sz[:, :], ALU.mult, ALU.mult).then_inc(dve_done, 1)
                    if kind == "glo":
                        dve.wait_ge(act_done, at("act", "ghi", a[0]))
                        return tt(g_lo[:, :], sz[:, :], g_hi[:, :].bitcast(f32), ALU.subtract).then_inc(dve_done, 1)
                    if kind == "bmul":
                        name, c = a[0], int(a[0][2])
                        dve.wait_ge(pe_done, at("pe", "tile", LAST[UIDX[name]]))
                        dve.wait_ge(act_done, at("act", "gate", "G" + name[1:]))
                        if name[1] != "A" and name != "bC0":
                            dve.wait_ge(pool_done, at("pool", "add" + {"bC1": "C0", "bB0": "C1", "bB1": "B0"}[name]))
                        for t in range(2):
                            cols = slice(t * D + c * 512, t * D + (c + 1) * 512)
                            o = merged[:, cols] if name[1] == "A" else tmp[:, t * 512:(t + 1) * 512]
                            last = stt(o, gate[:, cols], 1.0, pbank(name, t)[:, :], ALU.add, ALU.mult)
                        return last.then_inc(dve_done, 1)
                    if kind == "res":
                        name, c = a[0], int(a[0][1])
                        dve.wait_ge(pe_done, at("pe", "tile", LAST[UIDX[name]]))
                        for t in range(2):
                            o = xres[:, t * D + c * 512:t * D + (c + 1) * 512]
                            last = stt(o, o, ALPHA, pbank(name, t)[:, :], ALU.mult, ALU.add)
                        return last.then_inc(dve_done, 1)
                    if kind == "stats":
                        dve.wait_ge(dve_done, at("dve", "res", "o1"))
                        for i in range(4):
                            last = nc.vector.bn_stats(stat[:, i * 6:(i + 1) * 6], xres[:, i * 512:(i + 1) * 512])
                        last.then_inc(dve_chain, 1)
                        dve.wait_ge(dve_chain, link())
                        for t in range(2):
                            last = nc.vector.bn_aggr(agg[:, 2 * t:2 * t + 2], stat[:, t * 12:(t + 1) * 12])
                        last.then_inc(dve_chain, 1)
                        dve.wait_ge(dve_chain, link())
                        return ts(rstd[:, :], agg[:, :].rearrange("p (t two) -> p t two", two=2)[:, :, 1], LN_EPS, None, ALU.add).then_inc(dve_done, 1)
                    if kind == "norm":
                        t = a[0]
                        dve.wait_ge(pool_done, at("pool", "rstd"))
                        dve.wait_ge(ln_in, l * 32 + 32)
                        o = xres[:, t * D:(t + 1) * D]
                        ts(o, o, agg[:, 2 * t:2 * t + 1], rstd[:, t:t + 1], ALU.subtract, ALU.mult).then_inc(dve_chain, 1)
                        dve.wait_ge(dve_chain, link())
                        tt(o, o, lnp[:, 0:D], ALU.mult).then_inc(dve_chain, 1)
                        dve.wait_ge(dve_chain, link())
                        return tt(o, o, lnp[:, D:2 * D], ALU.add).then_inc(dve_done, 1)
                    raise ValueError(kind)

                for i, (_, *m) in enumerate(DVE_ORDER):
                    if i and m[0] != "lo":
                        dve.wait_ge(dve_done, at("dve", *DVE_ORDER[i - 1][1:]))
                    run(*m)
                assert links[0] == LINKS["dve"], links

        @block.gpsimd
        def _(pool):
            tt = nc.gpsimd.tensor_tensor
            pool.wait_ge(angles_ready, 1)
            for l in range(DEPTH):
                at = counter(l)
                link, links = linker("pool", l)

                def run(kind):
                    if kind == "zero":
                        if l:
                            pool.wait_ge(dve_done, at("dve", "norm", 1, back=True))
                        nc.gpsimd.memset(T[:, :], 0.0).then_inc(pool_chain, 1)
                        pool.wait_ge(pool_chain, link())
                        return nc.gpsimd.memset(TT[:, :], 0.0).then_inc(pool_done, 1)
                    if kind == "cx":
                        pool.wait_ge(dve_done, at("dve", "scan"))
                        return tt(ld, cum, ld, ALU.subtract).then_inc(pool_done, 1)
                    if kind in ("rnk", "rny"):
                        pool.wait_ge(dve_done, at("dve", "nss", kind[2]))
                        return tt(rn[:, :], ss[:, :], mhalf[:, :], ALU.pow).then_inc(pool_done, 1)
                    if kind == "arr":
                        pool.wait_ge(act_done, at("act", "ei"))
                        pool.wait_ge(dve_done, at("dve", "shift", "r"))
                        o = ar[:, :].rearrange("p (n two t) -> p n two t", two=2, t=CH)[:, :, 1, :]
                        return tt(o, r_t.rearrange("p (n t) -> p n t", t=CH), cum.rearrange("p (n t) -> p n t", t=CH), ALU.mult).then_inc(pool_done, 1)
                    if kind == "rk":
                        pool.wait_ge(dve_done, at("dve", "k2"))
                        return tt(tmp[:, :], r_t, k_t[:, :], ALU.mult).then_inc(pool_done, 1)
                    if kind == "kt":
                        pool.wait_ge(act_done, at("act", "en"))
                        pool.wait_ge(pool_done, at("pool", "rk"))
                        return tt(k_t[:, :], k_t[:, :], en[:, :], ALU.mult).then_inc(pool_done, 1)
                    if kind in ("lm1", "lm2"):
                        if kind == "lm1":
                            pool.wait_ge(dve_done, at("dve", "rs", 1, 1, 1))
                            if l:
                                pool.wait_ge(dve_done, at("dve", "norm", 1, back=True))
                        else:
                            pool.wait_ge(act_done, at("act", "w1", 1, 1))
                        mask = cst[:, (C_M16 if kind == "lm1" else C_M32):(C_M16 if kind == "lm1" else C_M32) + CH]
                        return tt(LM[:, :].rearrange("p (n c) -> p n c", c=CH), scm[:, :].rearrange("p (n c) -> p n c", c=256)[:, :, 0:CH],
                                  mask.unsqueeze(1).to_broadcast([P, 16, CH]), ALU.mult).then_inc(pool_done, 1)
                    if kind == "states":
                        pool.wait_ge(pe_done, at("pe", "sc", "C", 5))
                        nc.gpsimd.memset(q_tr[:, :], 0.0)
                        return nc.gpsimd.memset(k_tr[:, 0:512], 0.0).then_inc(pool_done, 1)
                    if kind == "rstd":
                        pool.wait_ge(dve_done, at("dve", "stats"))
                        return tt(rstd[:, :], rstd[:, :], mhalf[:, 0:2], ALU.pow).then_inc(pool_done, 1)
                    c = int(kind[4])
                    pool.wait_ge(dve_done, at("dve", "bmul", "b" + kind[3:]))
                    for t in range(2):
                        o = merged[:, t * D + c * 512:t * D + (c + 1) * 512]
                        last = tt(o, o, tmp[:, t * 512:(t + 1) * 512], ALU.add)
                    return last.then_inc(pool_done, 1)

                for i, (_, m) in enumerate(POOL_ORDER):
                    if i:
                        pool.wait_ge(pool_done, at("pool", POOL_ORDER[i - 1][1]))
                    run(m)
                assert links[0] == LINKS["pool"], links


def kernel(**inputs):
    import concourse.bacc as bacc
    from concourse.bass_utils import run_bass_kernel_spmd

    nc = bacc.Bacc("TRN2", target_bir_lowering=False, num_devices=1, dynamic_dma_scratch_size=1024)
    arrays, args = {}, []
    for name in INPUTS:
        a = np.ascontiguousarray(constants() if name == "consts" else inputs[name])
        arrays[f"in_{name}"] = a
        args.append(nc.dram_tensor(f"in_{name}", a.shape, mybir.dt.from_np(a.dtype), kind="ExternalInput").ap())
    args.append(nc.dram_tensor("out_x", (1, SEQ, D), mybir.dt.float32, kind="ExternalOutput").ap())
    hybrid_trunk(nc, *args)
    r = run_bass_kernel_spmd(nc, [arrays], core_ids=[0])
    return r.results[0]["out_x"]
```

```python
import math
from contextlib import ExitStack

import numpy as np

import concourse.bass as bass
from concourse import mybir

P = 128
D = 1024
SEQ = 256
DEPTH = 2
HD = 64
H = 8
W5 = 512
KT = D // P
ALPHA = (2 * DEPTH) ** 0.25
DECAY_SCALE = math.exp(-0.5)
GN_EPS = HD * 1e-5
LN_EPS = 1e-5
SCALE = HD ** -0.5
CH = 64
NC = SEQ // CH
NVEC = 17 + 28
RAW, SPL = 4, 4
HALVED = SPL
ROUND = 1.5 * 2.0 ** 23
TWO_PI = (6.28125, 0.0019350051879882812, 2 * math.pi - 6.28125 - 0.0019350051879882812)
PI_MAX = 3.1415925
INPUTS = ("x", "positions", "w_in", "mu_rwkv", "w0", "w_up", "a0", "a_up", "k_k", "k_a", "r_k", "gn_g", "gn_b", "sinks",
          "w_branch_a", "w_branch_b", "w_branch_c", "w_out", "ln_g", "ln_b", "consts")
LEAD = 3

C_ID, C_BO, C_CEN = 0, 128, 256
C_MSK = 384
C_M16, C_M32 = 512, 576
C_RST = 640
C_INV = C_RST + SEQ
C_SEL2 = C_INV + 32
C_SEL8 = C_SEL2 + 2
C_EYE16 = C_SEL8 + 512
C_NEG = C_EYE16 + 256
C_ALL = C_NEG + 256

UNITS = [
    ("Aq", "N", "w_in", 0, W5, 8), ("r", "T", "w_in", 2048, W5, 8), ("lora", "T", "w_in", 3584, 128, 8),
    ("k", "T", "w_in", 2560, W5, 8), ("v", "T", "w_in", 3072, W5, 8), ("Ak", "N", "w_in", 512, W5, 8),
    ("Av", "N", "w_in", 1024, W5, 8), ("Cq", "N", "w_in", 4224, W5, 8), ("Ckv", "N", "w_in", 4736, 256, 8),
    ("zA", "T", "w_in", 1536, W5, 8), ("GA0", "N", "w_in", 5504, W5, 8), ("GA1", "N", "w_in", 6016, W5, 8),
    ("bA0", "N", "w_branch_a", 0, W5, 4), ("bA1", "N", "w_branch_a", 512, W5, 4),
    ("zC", "T", "w_in", 4992, W5, 8), ("GC0", "N", "w_in", 7552, W5, 8), ("GC1", "N", "w_in", 8064, W5, 8),
    ("zB", "T", "w_in", 3712, W5, 8), ("bC0", "N", "w_branch_c", 0, W5, 4), ("bC1", "N", "w_branch_c", 512, W5, 4),
    ("GB0", "N", "w_in", 6528, W5, 8), ("bB0", "N", "w_branch_b", 0, W5, 4),
    ("GB1", "N", "w_in", 7040, W5, 8), ("bB1", "N", "w_branch_b", 512, W5, 4),
    ("o0", "N", "w_out", 0, W5, 8), ("o1", "N", "w_out", 512, W5, 8),
]
UIDX = {u[0]: i for i, u in enumerate(UNITS)}
TILES = []
for _u, (_n, _lay, _src, _c, _w, _k) in enumerate(UNITS[:-2]):
    _step = {128: 4, 256: 4, W5: 2}[_w]
    TILES += [(_u, _k0, _step) for _k0 in range(0, _k, _step)]
TILES += [(_u, _k0 + _i, 2) for _k0 in (0, 4) for _u in (len(UNITS) - 2, len(UNITS) - 1) for _i in (0, 2)]
NT = len(TILES)
assert NT % RAW == 0 and NT % SPL == 0 and len(UNITS) % 2 == 0
LAST = {u: max(n for n, t in enumerate(TILES) if t[0] == u) for u in range(len(UNITS))}

def _attn(x, g0):
    out = []
    for g in range(6):
        out += [(g0 + 2 * g, "sc", x, g), (g0 + 2 * g + 2, "pt", x, g), (g0 + 2 * g + 3, "pv", x, g)]
    return out + [(g0 + 7, "ot", x, 0), (g0 + 15, "ot", x, 1)]


MIXED = ("lora", "r", "k", "v", "zB")
WORK = [(0, "vec")]
WORK += [(11, "dec", i) for i in range(2)] + [(11, "icl", i) for i in range(2)]
WORK += [(16, "nss", "k"), (18, "nrt", "k"), (19, "nrb", "k", 0), (19, "nrb", "k", 1)]
WORK += [(20, "vt", 0), (20, "vt", 1)]
WORK += [(7, "qt", "Aq", 0), (7, "qt", "Aq", 1), (24, "qt", "Ak", 0), (24, "qt", "Ak", 1)]
WORK += _attn("A", 24) + [(23, "bon", 0), (23, "bon", 1)]
WORK += [(24 + i // 2, "rs", i // 4, (i % 4) // 2, i % 2) for i in range(8)]
WORK += [(36, "qt", "Cq", 0), (36, "qt", "Cq", 1), (37, "qt", "Ck", 0), (37, "qt", "Ck", 1)] + _attn("C", 38)
for _i, (_c, _t) in enumerate([(c, t) for c in range(2) for t in range(2)]):
    WORK += [(38 + _i // 2, "w1", _c, _t), (41 + _i // 2, "t1", _c, _t), (42 + _i // 2, "tt1", _c, _t),
             (44 + _i // 2, "w2", _c, _t), (47 + _i // 2, "tt2", _c, _t)]
WORK += [(49, "bt", "b", 0), (49, "bt", "b", 1), (50, "bt", "k", 0), (50, "bt", "k", 1)]
for _c in range(NC):
    WORK += [(50 + 3 * _c, "cp", _c), (51 + 3 * _c, "cu", _c), (52 + 3 * _c, "cy", _c)]
    WORK += [(52 + 3 * _c, "cs", _c)] if _c < NC - 1 else []
WORK += [(63, "cen", 0), (63, "cen", 1), (64, "nss", "y"), (66, "nrt", "y"), (67, "nrb", "y", 0), (67, "nrb", "y", 1)]
WORK += [(76 + 6 * h, "mt", t, h) for h in range(2) for t in range(2)]
WORK += [(NT, "nxt", t, h) for t in range(2) for h in range(2)]
SHIFT = {
    ("bt", "b", 0): -0.5, ("bt", "b", 1): -0.5, ("bt", "k", 0): -1, ("bt", "k", 1): -1, ("cp", 0): -1, ("cs", 1): 0.5,
    ("cu", 0): -1, ("cu", 1): 0.5, ("cu", 2): 0.5, ("cu", 3): 0.5, ("icl", 1): 0.5, ("mt", 0, 1): -0.5, ("mt", 1, 1): -0.5,
    ("nrt", "y"): 0.5, ("nss", "k"): -1, ("ot", "A", 1): 1, ("ot", "C", 1): 0.5, ("pt", "C", 1): 1, ("pv", "A", 0): 1,
    ("pv", "C", 1): 1, ("pv", "C", 5): 0.5, ("rs", 0, 0, 0): 1, ("rs", 0, 0, 1): 1, ("rs", 0, 1, 0): 1.5,
    ("rs", 0, 1, 1): 1.5, ("rs", 1, 0, 0): 2.5, ("rs", 1, 0, 1): 2.5, ("rs", 1, 1, 0): 1.5, ("rs", 1, 1, 1): 1.5,
    ("sc", "A", 4): 0.5, ("sc", "C", 2): 1, ("t1", 0, 1): 0.5, ("tt1", 1, 0): 0.5, ("tt1", 1, 1): 0.5, ("tt2", 1, 0): -1,
    ("w1", 1, 0): 0.5, ("w1", 1, 1): 0.5, ("w2", 0, 0): 1, ("w2", 0, 1): 1, ("w2", 1, 0): 1, ("w2", 1, 1): 1,
}
DELAY = {
    ("act", "Av"): 1, ("act", "cp", 1): -1, ("act", "exp", "A", 1): 2, ("act", "exp", "A", 2): 1, ("act", "exp", "C", 1): 1,
    ("act", "gate", "GA0"): -1, ("act", "gate", "GA1"): -1, ("act", "gate", "GB0"): -1, ("act", "gate", "GC1"): -1,
    ("act", "ghi", "B"): 1, ("act", "ghi", "C"): 1, ("act", "icl", 1): 1, ("act", "pt", "A", 4): -2,
    ("act", "pt", "A", 5): -1, ("act", "qt", "Ak", 0): -1, ("dve", "bmul", "bB0"): -1, ("dve", "bmul", "bC1"): 1,
    ("dve", "bon", 0): -1, ("dve", "bon", 1): -1, ("dve", "cs", 0): -1, ("dve", "cu", 0): -1, ("dve", "g", "C"): -1,
    ("dve", "kb"): 1, ("dve", "max", "A", 1): -1, ("dve", "max", "A", 3): 1, ("dve", "max", "C", 0): -1,
    ("dve", "max", "C", 2): -1, ("dve", "nrb", "y", 0): -1, ("dve", "nrb", "y", 1): -1, ("dve", "nss", "k"): -1,
    ("dve", "pv", "A", 3): 1, ("dve", "pv", "A", 5): -1, ("dve", "rs", 0, 0, 0): -1, ("dve", "sub", 0): 1,
    ("dve", "sub", 1): 1, ("dve", "sub", 2): 1, ("dve", "sz", "B"): 1, ("dve", "ta"): -1, ("dve", "tt1", 1, 0): -1,
}
EARLY = dict(act=(4, 5, 14, 17, 22, 24, 27, 28, 31, 33, 37, 41, 42, 43, 44, 47, 49, 50, 52, 53, 54, 58, 59, 61, 65, 66, 68, 70, 71, 76, 77, 78, 84, 85),
             dve=(0, 3, 5, 9, 12, 17, 28, 40, 50, 51, 56, 62, 67, 70, 76, 78, 79, 85, 86))
BOUNCE = (35, 35, 40, 42)
WORK = sorted(((w[0] + SHIFT.get(w[1:], 0),) + w[1:] for w in WORK), key=lambda w: w[0])
WORK = [(math.floor(w[0]),) + w[1:] for w in WORK]
GAP = {w[1:]: w[0] for w in WORK}
WIDX = {w[1:]: i for i, w in enumerate(WORK)}


def release(w):
    kind = w[0]
    renamed = {"nxt": "nxtl", "mt": "mtl", "sc": "exp"}
    on_act = ("vec", "dec", "icl", "nrt", "vt", "qt", "sc", "pt", "ot", "w1", "w2", "bt", "cp", "cy", "cen")
    return ("act" if kind in on_act else "dve", (renamed.get(kind, kind),) + w[1:])


def unit_release(name):
    if name in MIXED:
        return "dve", ("shift", name)
    if name in ("Aq", "Ak", "Cq"):
        return "dve", ("rope", name, 1)
    if name == "Ckv":
        return "dve", ("ropek", 1)
    if name == "Av":
        return "act", ("Av",)
    if name[0] == "z":
        return "dve", ("sz", name[1])
    if name[0] == "G":
        return "act", ("gate", name)
    return "dve", (("bmul", name) if name[0] == "b" else ("res", int(name[1]), 1))



G_STEP = {"A": 41, "C": 55, "B": 69}


def _order(eng):
    out = []
    half = {"act": "hi", "dve": "lo"}[eng]
    for n in range(NT):
        for u, (name, *_r) in enumerate(UNITS):
            if LAST[u] == n - 2 and name == "zB":
                out += [(n, "ztanh" if eng == "act" else "sz", "B")]
            if LAST[u] != n - 1 or name[0] == "o":
                continue
            if eng == "act":
                out += [(n, "mix", name)] if name in MIXED else []
                out += [(n, "Av")] if name == "Av" else []
                out += [(n, "vc")] if name == "Ckv" else []
                out += [(n, "ztanh", name[1])] if name in ("zA", "zC") else []
                out += [(n, "gate", name)] if name[0] == "G" else []
                out += [(n, "ltanh")] if name == "lora" else []
                out += [(n, "ksq")] if name == "k" else []
            else:
                out += [(n, "shift", name)] if name in MIXED else []
                out += [(n, "rope", name, t) for t in range(2)] if name in ("Aq", "Ak", "Cq") else []
                out += [(n, "ropek", t) for t in range(2)] if name == "Ckv" else []
                out += [(n, "sz", name[1])] if name in ("zA", "zC") else []
                out += [(n, "bmul", name)] if name[0] == "b" else []
        for w in WORK:
            if w[0] == n - 1 and n > 0:
                if w[1] == "sc":
                    out += [(n, "exp" if eng == "act" else "max") + w[2:]]
                elif w[1] == "mt":
                    out += [(n, "mth" if eng == "act" else "mtl") + w[2:]]
                elif release(w[1:])[0] == eng:
                    out += [(n,) + w[1:]]
        if eng == "act":
            out += [(n, "en"), (n, "ex"), (n, "ei"), (n, "ec")] if n == 14 else []
            out += [(n, "ghi", x) for x in "ACB" if G_STEP[x] == n]
        else:
            out += {1: [(n, "derive")], 12: [(n, "ld"), (n, "scan")], 15: [(n, "ta")], 20: [(n, "k2"), (n, "ara")], 21: [(n, "kb")]}.get(n, [])
            out += [(n, "sub", n - 31)] if 31 <= n < 34 else []
            out += [(n, "gn")] if n == 68 else []
            for x in "ACB":
                out += [(n, "g", x), (n, "glo", x)] if G_STEP[x] == n else []
        if HALVED <= n + LEAD < NT:
            out += [(n, half, n + LEAD)]
    place = [(w[0] + DELAY.get((eng,) + w[1:], 0), 0 if w[1] != half else 2 * (w[0] not in EARLY[eng]) - 1) for w in out]
    out = [w for _, w in sorted(zip(place, out), key=lambda e: e[0])]
    if eng == "act":
        return out + [(NT, "nhi", 0), (NT, "nhi", 1), (NT, "nhi", 2), (NT, "nxth", 0, 0), (NT, "nhi", 3), (NT, "nxth", 0, 1),
                      (NT, "nxth", 1, 0), (NT, "nxth", 1, 1)]
    return out + [(NT, "res", 0, 0), (NT, "res", 1, 0), (NT, "agg", 0), (NT, "norm", 0, 0), (NT, "res", 0, 1), (NT, "norm", 0, 1),
                  (NT, "nxtl", 0, 0), (NT, "nlo", 3), (NT, "nxtl", 0, 1), (NT, "res", 1, 1), (NT, "agg", 1),
                  (NT, "norm", 1, 0), (NT, "norm", 1, 1), (NT, "nxtl", 1, 0), (NT, "nxtl", 1, 1)]


PE_ORDER = []
for _n in range(NT - HALVED):
    PE_ORDER += [(_n, "tile", _n)] + [w for w in WORK if w[0] == _n]
PE_ORDER += [(NT, "part", n) for n in range(NT - HALVED, NT)] + [(NT, "tile", n) for n in range(NT - HALVED, NT)]
PE_ORDER += [(NT, "nxt", 0, h) for h in range(2)] + [(NT, "npart", n) for n in range(HALVED)] + [(NT, "nxt", 1, h) for h in range(2)]
POOL_ORDER = [(0, k) for k in ("zero", "cx", "rnk", "arr", "rk", "kt", "lm1", "lm2", "states", "rny", "addC0", "addC1")]
POOL_ORDER += [(NT, "rstd", 0), (NT, "nlo", 0), (NT, "nlo", 1), (NT, "nlo", 2), (NT, "rstd", 1)]
ORDER = dict(pe=PE_ORDER, act=_order("act"), dve=_order("dve"), pool=POOL_ORDER)
NEXT = ("nxt", "npart", "nhi", "nlo", "nxth", "nxtl")
LINKS = dict(dve=95, pool=1)


HALVES = [(t, h) for t in range(2) for h in range(2)]
FIRST = dict(pe=[("nxt", *v) for v in HALVES] + [("npart", n) for n in range(HALVED)],
             act=[("nhi", 0), ("nxth", 0, 0), ("nhi", 1), ("nxth", 0, 1), ("nxth", 1, 0), ("nxth", 1, 1), ("nhi", 2), ("nhi", 3)],
             dve=[("nxtl", *v) for v in HALVES] + [("nlo", 3)], pool=[("nlo", n) for n in range(3)])


def steps(eng, l):
    if l < 0:
        return FIRST[eng]
    return [m[1:] for m in ORDER[eng] if l < DEPTH - 1 or m[1] not in NEXT]


START = {(eng, l): sum(len(steps(eng, k)) for k in range(-1, l)) for eng in ORDER for l in range(-1, DEPTH)}
COUNT = {(eng, l): {m: START[eng, l] + i + 1 for i, m in enumerate(steps(eng, l))} for eng in ORDER for l in range(-1, DEPTH)}

def constants():
    c = np.zeros((P, C_ALL), np.float32)
    i = np.arange(P)
    c[:, C_ID:C_ID + P] = np.eye(P)
    same = (i[:, None] // HD) == (i[None, :] // HD)
    c[:, C_BO:C_BO + P] = same
    c[:, C_CEN:C_CEN + P] = np.eye(P) - same / HD
    s, t = (i % CH)[:, None], np.arange(CH)[None, :]
    c[:, C_MSK:C_MSK + CH] = s < t
    c[:, C_MSK + CH:C_MSK + 2 * CH] = s <= t
    c[:, C_M16:C_M16 + CH] = (s // 32 == t // 32) & (s // 16 != t // 16)
    c[:, C_M32:C_M32 + CH] = s // 32 != t // 32
    c[:, C_RST:C_RST + SEQ] = (np.arange(SEQ) % CH != 0)
    half = HD // 2
    c[:, C_INV:C_INV + half] = np.power(np.float32(10000.0), -np.arange(half, dtype=np.float32) / half)
    c[:, C_SEL2] = i < HD
    c[:, C_SEL2 + 1] = i >= HD
    for j in range(4):
        for h in range(2):
            c[2 * j + h, C_SEL8 + j * P + h * HD:C_SEL8 + j * P + (h + 1) * HD] = 1
    c[:, C_EYE16:C_EYE16 + 256] = np.eye(16).reshape(-1)
    q, k = i[:, None], i[None, :]
    c[:, C_NEG:C_NEG + P] = np.where(k <= q, 0, -1e30)
    c[:, C_NEG + P:C_NEG + 2 * P] = np.where(k > q, 0, -1e30)
    return c


def hybrid_trunk(nc, x, positions, w_in, mu_rwkv, w0, w_up, a0, a_up, k_k, k_a, r_k, gn_g, gn_b, sinks,
                 w_branch_a, w_branch_b, w_branch_c, w_out, ln_g, ln_b, consts, out):
    f32, f32r, bf16, i32 = mybir.dt.float32, mybir.dt.float32r, mybir.dt.bfloat16, mybir.dt.int32
    ACT, ALU, AX = mybir.ActivationFunctionType, mybir.AluOpType, mybir.AxisListType
    weights = dict(w_in=w_in, w_branch_a=w_branch_a, w_branch_b=w_branch_b, w_branch_c=w_branch_c, w_out=w_out)

    blocks = nc.dram_tensor("blocks", (P, 256), f32, kind="Internal").ap()
    inverses = nc.dram_tensor("inverses", (P, 512), f32, kind="Internal").ap()

    with ExitStack() as ctx:
        def sb(name, cols, dt=f32, rows=P):
            return ctx.enter_context(nc.sbuf_tensor(name, [rows, cols], dt))

        raw = sb("raw", RAW * 1024)
        w_hi, w_lo = sb("w_hi", SPL * 1024, f32r), sb("w_lo", SPL * 1024, f32r)
        xres = sb("xres", 2 * D)
        xt_hi, xt_lo = sb("xt_hi", KT * SEQ, f32r), sb("xt_lo", KT * SEQ, f32r)
        g_hi, g_lo = sb("g_hi", 4 * SEQ, f32r), sb("g_lo", 4 * SEQ, f32r)
        o_A, o_C = sb("o_A", 4 * SEQ), sb("o_C", 4 * SEQ)
        gate, merged, sz, tmp = sb("gate", 2 * D), sb("merged", 2 * D), sb("sz", 1024), sb("tmp", 1024)
        r_t, ld = gate[:, 0:1024], gate[:, 1024:2048]
        iclr, cum, en = merged[:, 0:1024], merged[:, 1024:2048], sz
        lnp = gate
        k_t, b_t, v_t, ar = sb("k_t", 1024), sb("b_t", 1024), sb("v_t", 1024), sb("ar", 2048)
        vtok, lora, scm = sb("vtok", 1024), sb("lora", SEQ), sb("scm", 4096)
        T, TT, Wb, LM = sb("T", 1024), sb("TT", 1024), sb("Wb", 1024), sb("LM", 1024)
        btok, ktok, yt = T, LM, Wb
        lb, X, XT, subt = tmp[:, 0:256], tmp[:, 256:512], tmp[:, 512:768], tmp[:, 768:1024]
        up, bor = sb("up", W5), sb("bor", W5)
        q_tr, k_tr, v_a = sb("q_tr", 1024), sb("k_tr", 1024), sb("v_a", 1024)
        v_c, roped, rswap, kdup = sb("v_c", 256), sb("roped", 1024), sb("rswap", 512), sb("kdup", 512)
        prob, pT, otok = sb("prob", 1024), sb("pT", 1024), sb("otok", 512)
        S = [None, q_tr[:, 0:512], q_tr[:, 512:1024], k_tr[:, 0:512]]
        pch, uch, ysq = k_tr[:, 512:1024], v_a, pT
        cst, rot = sb("cst", C_ALL), sb("rot", 2 * 128)
        ang, turn = sb("ang", 128), sb("turn", 128)
        pos_i, pos_f = sb("pos_i", 2, i32), sb("pos_f", 2)
        id_bf, neg_bf = sb("id_bf", P, bf16), sb("neg_bf", 256, bf16)
        vrow, vcol = sb("vrow", P, rows=NVEC), sb("vcol", NVEC)
        omu, halves, sink, nsink = sb("omu", 17), sb("halves", 12), sb("sink", H), sb("nsink", H)
        mx, nb, den, rec, esk = sb("mx", 8), sb("nb", 8), sb("den", 8), sb("rec", 8), sb("esk", 8)
        ss, rn, mhalf, ec = sb("ss", 16), sb("rn", 16), sb("mhalf", 16), sb("ec", 16)
        rnt = sb("rnt", SEQ, rows=8)
        stat, agg, rstd = sb("stat", 24), sb("agg", 4), sb("rstd", 2)

        pb = [ctx.enter_context(nc.psum_tensor(f"pb{i}", [P, W5], f32)) for i in range(4)]
        wb = [ctx.enter_context(nc.psum_tensor(f"wb{i}", [P, W5], f32)) for i in range(4)]

        def sem(name):
            return ctx.enter_context(nc.semaphore(name))

        pe_done, act_done, dve_done, pool_done = sem("pe_done"), sem("act_done"), sem("dve_done"), sem("pool_done")
        done = dict(act=act_done, dve=dve_done, pool=pool_done)
        dve_chain, pool_chain = sem("dve_chain"), sem("pool_chain")
        cst_in, pos_in, vec_in, up_in, sink_in, ln_in = (sem(n) for n in ("cst_in", "pos_in", "vec_in", "up_in", "sink_in", "ln_in"))
        ident_in, x_in = sem("ident_in"), [sem("x_in0"), sem("x_in1")]
        x_out, lb_out, lb_in, t_out, t_in = (sem(n) for n in ("x_out", "lb_out", "lb_in", "t_out", "t_in"))
        raw_in = [sem(f"raw_in{i}") for i in range(RAW)]
        bf_ready, angles_ready, rot_ready, pos_ready = sem("bf_ready"), sem("angles_ready"), sem("rot_ready"), sem("pos_ready")

        ident, head_ones, centre = cst[:, C_ID:C_ID + P], cst[:, C_BO:C_BO + P], cst[:, C_CEN:C_CEN + P]
        MU, W0, A0, KK_, KA, RK_, GG, GB = 0, 17, 21, 25, 29, 33, 37, 41
        MUROW = {"lora": 12, "r": 0, "k": 4, "v": 8, "zB": 13}
        TDST = {"lora": lora, "r": r_t, "k": k_t, "v": v_t, "zB": k_t}

        def vec(row, j):
            return vcol[:, row + j:row + j + 1]

        def jt(buf, j, t=None):
            return buf[:, j * SEQ:(j + 1) * SEQ] if t is None else buf[:, j * SEQ + t * P:j * SEQ + (t + 1) * P]

        def cut(buf, t):
            return buf.rearrange("p (j t c) -> p j t c", t=2, c=P)[:, :, t, :]

        def col4(b, n=4):
            return b[:, 0:n * P].rearrange("p (j c) -> p j c", j=n)

        def slot(n):
            return slice((n % SPL) * 1024, (n % SPL) * 1024 + TILES[n][2] * UNITS[TILES[n][0]][4])

        def rslot(n):
            return slice((n % RAW) * 1024, (n % RAW) * 1024 + TILES[n][2] * UNITS[TILES[n][0]][4])

        def wbank(*w):
            return wb[WIDX[w] % 4]

        def pbank(unit, t):
            return pb[(UIDX[unit] % 2) * 2 + t]

        def z_part(x_, t):
            return k_t[:, t * 512:(t + 1) * 512] if x_ == "B" else pbank("z" + x_, t)[:, :]

        def nlo_on(n):
            return "dve" if n == 3 else "pool"

        def heads_of(g):
            return (0, [g + 2 * i for i in range(4)]) if g < 2 else (1, [(g - 2) % 2 + 4 * ((g - 2) // 2) + 2 * i for i in range(2)])

        def rows(c):
            return slice(64 * (c % 2), 64 * (c % 2) + 64)

        def sco(h, t, part):
            o = ((t * 2 + h % 2) * 4 + h // 2) * 256 + 64 * part
            return slice(o, o + 64)

        def inv(h, t):
            o = (t * 8 + (h % 2) * 4 + h // 2) * CH
            return slice(o, o + CH)

        def counter(l):
            def at(eng, *m, back=False):
                return COUNT[eng, l - 1 if back else l][m]
            return at

        def linker(name, l):
            n = [0]

            def link():
                n[0] += 1
                return l * LINKS[name] + n[0]
            return link, n

        block = ctx.enter_context(nc.Block())

        @block.sync
        def _(sp):
            for t in range(2):
                sp.dma_start(xres[:, t * D:(t + 1) * D], x[0, t * P:(t + 1) * P, :]).then_inc(x_in[t], 16)
                if t == 0:
                    sp.dma_start(ident, consts[:, C_ID:C_ID + P]).then_inc(ident_in, 16)
            for l in range(DEPTH):
                at = counter(l)
                ly = slice(l, l + 1)
                for n, (u, k0, kn) in enumerate(TILES):
                    _, _, src, c0, width, _ = UNITS[u]
                    if n == 4:
                        if l == 0:
                            sp.dma_start(cst[:, P:], consts[:, P:]).then_inc(cst_in, 16)
                            for t in range(2):
                                sp.dma_start(pos_i[:, t:t + 1], positions[0, t * P:(t + 1) * P].unsqueeze(1)).then_inc(pos_in, 16)
                        if l:
                            sp.wait_ge(act_done, at("act", "exp", "C", 5, back=True))
                            sp.wait_ge(dve_done, at("dve", "max", "C", 5, back=True))
                            sp.wait_ge(dve_done, at("dve", "gn", back=True))
                        sp.dma_start(vrow[0:17, :], mu_rwkv[ly, :].rearrange("a (r c) -> (a r) c", c=P)).then_inc(vec_in, 16)
                        for i, v in ((0, w0), (1, a0), (2, k_k), (3, k_a), (5, gn_g), (6, gn_b)):
                            sp.dma_start(vrow[17 + 4 * i:21 + 4 * i, :], v[ly, :].rearrange("a (r c) -> (a r) c", c=P)).then_inc(vec_in, 16)
                        sp.dma_start(vrow[33:37, :], r_k[ly, :, :].rearrange("a (r two) c -> (a r) (two c)", two=2)).then_inc(vec_in, 16)
                        sp.dma_start(up[0:64, :], w_up[ly, :, :].rearrange("a p n -> (a p) n")).then_inc(up_in, 16)
                        sp.dma_start(up[64:128, :], a_up[ly, :, :].rearrange("a p n -> (a p) n")).then_inc(up_in, 16)
                        sp.dma_start(sink[:, :], sinks[ly, :].rearrange("a h -> (a h)").partition_broadcast(P)).then_inc(sink_in, 16)
                    if n == BOUNCE[0]:
                        sp.wait_ge(dve_done, at("dve", "rs", 1, 1, 1))
                        for blk in range(8):
                            r0, c16 = 16 * blk, 16 * (blk % 4)
                            sp.dma_start(blocks[blk * 16:blk * 16 + 16, :].rearrange("n (s c) -> s n c", c=16),
                                         scm[r0:r0 + 16, :].rearrange("p (n c) -> p n c", c=256)[:, :, c16:c16 + 16]).then_inc(lb_out, 16)
                    if n == BOUNCE[1]:
                        sp.wait_ge(lb_out, l * 128 + 128)
                        sp.dma_start(lb, blocks[:, :]).then_inc(lb_in, 16)
                    if n == BOUNCE[2]:
                        sp.wait_ge(dve_done, at("dve", "sub", 2))
                        sp.dma_start(inverses[:, :], tmp[:, 256:768]).then_inc(t_out, 16)
                    if n == BOUNCE[3]:
                        sp.wait_ge(t_out, l * 16 + 16)
                        sp.wait_ge(pool_done, at("pool", "zero"))
                        for i, dst in enumerate((T, TT)):
                            for blk in range(8):
                                r0, c16 = 16 * blk, 16 * (blk % 4)
                                sp.dma_start(dst[r0:r0 + 16, :].rearrange("p (n c) -> p n c", c=CH)[:, :, c16:c16 + 16],
                                             inverses[blk * 16:blk * 16 + 16, i * 256:(i + 1) * 256].rearrange("n (t c) -> t n c", c=16))\
                                    .then_inc(t_in, 16)
                    if n >= RAW + HALVED:
                        sp.wait_ge(act_done, at("act", "hi", n - RAW))
                        sp.wait_ge(dve_done, at("dve", "lo", n - RAW))
                    elif n >= RAW:
                        sp.wait_ge(act_done, at("act", "nhi", n - RAW, back=True))
                        sp.wait_ge(done[nlo_on(n - RAW)], at(nlo_on(n - RAW), "nlo", n - RAW, back=True))
                    elif l:
                        sp.wait_ge(act_done, at("act", "hi", NT + n - RAW, back=True))
                        sp.wait_ge(dve_done, at("dve", "lo", NT + n - RAW, back=True))
                    sp.dma_start(raw[:, rslot(n)].rearrange("p (k c) -> p k c", c=width),
                                 weights[src][ly, k0 * P:(k0 + kn) * P, c0:c0 + width]
                                 .rearrange("a (k p) c -> p (a k) c", p=P)).then_inc(raw_in[n % RAW], 16)
                sp.wait_ge(dve_done, at("dve", "bmul", "bB1"))
                sp.dma_start(lnp[:, 0:D], ln_g[ly, :].rearrange("a h -> (a h)").partition_broadcast(P)).then_inc(ln_in, 16)
                sp.dma_start(lnp[:, D:2 * D], ln_b[ly, :].rearrange("a h -> (a h)").partition_broadcast(P)).then_inc(ln_in, 16)
            for t in range(2):
                for h in range(2):
                    sp.wait_ge(dve_done, at("dve", "norm", t, h))
                    sp.dma_start(out[0, t * P:(t + 1) * P, h * 512:(h + 1) * 512],
                                 xres[:, t * D + h * 512:t * D + (h + 1) * 512]).then_inc(x_out, 16)
            sp.wait_ge(x_out, 64)

        @block.tensor
        def _(pe):
            mm, tr = nc.tensor.matmul, nc.tensor.transpose
            pe.wait_ge(ident_in, 16)
            for l in range(-1, DEPTH):
                at = counter(l)

                def fill(w):
                    i, kind, a = WIDX[w], w[0], w[1:]
                    b = wb[i % 4]
                    if l >= 0 and i >= 4:
                        e, m = release(WORK[i - 4][1:])
                        pe.wait_ge(done[e], at(e, *m))
                    elif l >= 0:
                        e, m = release([v for v in WORK if WIDX[v[1:]] % 4 == i][-1][1:])
                        pe.wait_ge(done[e], at(e, *m, back=True))
                    if kind == "nxt":
                        t, h = a
                        if l < 0:
                            pe.wait_ge(x_in[t], 16)
                        else:
                            pe.wait_ge(dve_done, at("dve", "norm", t, h))
                        for q in range(4):
                            last = tr(b[:, q * P:(q + 1) * P], xres[:, t * D + (4 * h + q) * P:t * D + (4 * h + q + 1) * P], ident)
                    elif kind == "vec":
                        pe.wait_ge(vec_in, l * 128 + 128)
                        pe.wait_ge(cst_in, 16)
                        last = tr(b[:, 0:NVEC], vrow[:, :], cst[0:NVEC, C_ID:C_ID + NVEC])
                    elif kind in ("dec", "icl"):
                        p0 = 0 if kind == "dec" else 64
                        pe.wait_ge(up_in, l * 32 + 32)
                        pe.wait_ge(act_done, at("act", "ltanh"))
                        for q in range(2):
                            last = mm(b[:, q * SEQ:(q + 1) * SEQ], up[p0:p0 + 64, (2 * a[0] + q) * P:(2 * a[0] + q + 1) * P],
                                      lora[p0:p0 + 64, :], start=True, stop=True)
                    elif kind == "nss":
                        src = b_t if a[0] == "k" else ysq
                        pe.wait_ge(act_done, at("act", *(("ksq",) if a[0] == "k" else ("cen", 1))))
                        for t in range(2):
                            for j in range(4):
                                last = mm(b[:, t * 8 + 2 * j:t * 8 + 2 * j + 2], jt(src, j, t), cst[:, C_SEL2:C_SEL2 + 2], start=True, stop=True)
                    elif kind == "nrt":
                        pe.wait_ge(pool_done, at("pool", "rn" + a[0]))
                        for t in range(2):
                            last = tr(b[0:8, t * P:(t + 1) * P], rn[:, t * 8:(t + 1) * 8], ident)
                    elif kind == "nrb":
                        pe.wait_ge(act_done, at("act", "nrt", a[0]))
                        for q in range(2):
                            j = 2 * a[1] + q
                            last = mm(b[:, q * SEQ:(q + 1) * SEQ], cst[0:8, C_SEL8 + j * P:C_SEL8 + (j + 1) * P], rnt[:, :],
                                      start=True, stop=True)
                    elif kind == "vt":
                        pe.wait_ge(dve_done, at("dve", "shift", "v"))
                        for j in range(4):
                            last = tr(b[:, j * P:(j + 1) * P], jt(v_t, j, a[0]), ident)
                    elif kind == "bt":
                        for j in range(4):
                            last = tr(b[:, j * P:(j + 1) * P], jt(b_t if a[0] == "b" else k_t, j, a[1]), ident)
                    elif kind == "bon":
                        pe.wait_ge(pool_done, at("pool", "rk"))
                        for q in range(2):
                            j = 2 * a[0] + q
                            last = mm(b[:, q * SEQ:(q + 1) * SEQ], bor[:, j * P:(j + 1) * P], jt(tmp, j), start=True, stop=True)
                    elif kind == "qt":
                        t = a[1]
                        if a[0] == "Ck":
                            pe.wait_ge(dve_done, at("dve", "ropek", t))
                            for n2 in range(2):
                                last = tr(b[:, n2 * P:(n2 + 1) * P], kdup[:, t * 256 + n2 * P:t * 256 + (n2 + 1) * P], ident)
                        else:
                            pe.wait_ge(dve_done, at("dve", "rope", a[0], t))
                            for j in range(4):
                                last = tr(b[:, j * P:(j + 1) * P], roped[:, t * W5 + j * P:t * W5 + (j + 1) * P], ident)
                    elif kind == "sc":
                        t, hs = heads_of(a[1])
                        keys = P * (t + 1)
                        pe.wait_ge(bf_ready, 2)
                        pe.wait_ge(act_done, at("act", "qt", a[0] + "k", 1))
                        for i2, h in enumerate(hs):
                            p0, j = 64 * (h % 2), h // 2
                            kj = j if a[0] == "A" else h // 4
                            mm(b[:, i2 * keys:(i2 + 1) * keys], q_tr[p0:p0 + 64, j * SEQ + t * P:j * SEQ + (t + 1) * P],
                               k_tr[p0:p0 + 64, kj * SEQ:kj * SEQ + keys], start=(i2 == 0), stop=False, skip_group_check=True)
                        for i2, h in enumerate(hs):
                            if t == 1 and a[0] == "C":
                                mm(b[:, i2 * keys:i2 * keys + P], id_bf[:, :], neg_bf[:, P:2 * P], start=False, stop=False, skip_group_check=True)
                            last = mm(b[:, (i2 + 1) * keys - P:(i2 + 1) * keys], id_bf[:, :], neg_bf[:, 0:P], start=False,
                                      stop=(i2 == len(hs) - 1), skip_group_check=True)
                    elif kind == "pt":
                        pe.wait_ge(act_done, at("act", "exp", *a))
                        for q in range(4):
                            o = (a[1] % 2) * 512 + q * P
                            last = tr(b[:, q * P:(q + 1) * P], prob[:, o:o + P], ident)
                    elif kind == "pv":
                        t, hs = heads_of(a[1])
                        pe.wait_ge(act_done, at("act", "pt", *a))
                        pe.wait_ge(act_done, at("act", *(("Av",) if a[0] == "A" else ("vc",))))
                        for i2, h in enumerate(hs):
                            for kb in range(t + 1):
                                o = (a[1] % 2) * 512 + (i2 * (t + 1) + kb) * P
                                v = v_a[:, kb * W5 + h * HD:kb * W5 + (h + 1) * HD] if a[0] == "A" else \
                                    v_c[:, kb * P + (h // 4) * HD:kb * P + (h // 4 + 1) * HD]
                                last = mm(b[:, i2 * HD:(i2 + 1) * HD], pT[:, o:o + P], v, start=(kb == 0), stop=(kb == t))
                    elif kind == "ot":
                        pe.wait_ge(dve_done, at("dve", "pv", a[0], 1 if a[1] == 0 else 5))
                        for j in range(4):
                            last = tr(b[:, j * P:(j + 1) * P], otok[:, j * P:(j + 1) * P], ident)
                    elif kind == "rs":
                        t, par, half = a
                        pe.wait_ge(pool_done, at("pool", "kt"))
                        pe.wait_ge(dve_done, at("dve", "kb"))
                        p0 = 64 * par
                        for i2 in range(2):
                            j = 2 * half + i2
                            for c in (2 * t, 2 * t + 1):
                                for q, src in enumerate((b_t, k_t)):
                                    last = mm(b[rows(c), i2 * 256 + q * 128:i2 * 256 + (q + 1) * 128],
                                              src[p0:p0 + 64, j * SEQ + c * CH:j * SEQ + (c + 1) * CH],
                                              ar[p0:p0 + 64, (j * NC + c) * 128:(j * NC + c + 1) * 128], start=True, stop=True)
                    elif kind in ("w1", "w2", "t1", "tt1", "tt2"):
                        cp, t = a
                        r = rows(cp)
                        lhs, rhs = {"w": (LM, T), "t": (TT, Wb), "tt": (Wb, TT)}[kind[:-1]]
                        if kind == "w1":
                            pe.wait_ge(t_in, l * 256 + 256)
                            pe.wait_ge(pool_done, at("pool", "lm1"))
                        elif kind == "w2":
                            pe.wait_ge(pool_done, at("pool", "lm2"))
                            pe.wait_ge(dve_done, at("dve", "t1", 1, 1))
                        elif kind == "tt2":
                            pe.wait_ge(act_done, at("act", "w2", 1, 1))
                            pe.wait_ge(dve_done, at("dve", "tt1", 1, 1))
                        else:
                            pe.wait_ge(act_done, at("act", "w1", 1, 1))
                        for h in range(8):
                            o = slice((t * 8 + h) * CH, (t * 8 + h + 1) * CH)
                            last = mm(b[r, h * CH:(h + 1) * CH], lhs[r, o], rhs[r, o], start=True, stop=True)
                    elif kind == "cp":
                        c, t, r = a[0], a[0] // 2, rows(a[0])
                        pe.wait_ge(act_done, at("act", "vt", 1))
                        if c > 0:
                            pe.wait_ge(dve_done, at("dve", "cs", c - 1))
                            for j in range(4):
                                mm(b[r, j * P:(j + 1) * P], ar[:, (j * NC + c) * 128:(j * NC + c) * 128 + 64],
                                   S[c][:, j * P:(j + 1) * P], start=(j == 0), stop=False, skip_group_check=True)
                        for h in range(8):
                            last = mm(b[r, h * HD:(h + 1) * HD], scm[r, sco(h, t, 2)], vtok[r, t * W5 + h * HD:t * W5 + (h + 1) * HD],
                                      start=(c == 0 and h == 0), stop=(h == 7), skip_group_check=True)
                    elif kind == "cu":
                        c, t, r = a[0], a[0] // 2, rows(a[0])
                        pe.wait_ge(act_done, at("act", "cp", c))
                        pe.wait_ge(dve_done, at("dve", "tt2", 1, 1))
                        for h in range(8):
                            last = mm(b[r, h * HD:(h + 1) * HD], TT[r, inv(h, t)], pch[r, h * HD:(h + 1) * HD], start=True, stop=True)
                    elif kind == "cs":
                        c, t, r = a[0], a[0] // 2, rows(a[0])
                        pe.wait_ge(dve_done, at("dve", "cu", c))
                        pe.wait_ge(act_done, at("act", "bt", "k", 1))
                        for j in range(4):
                            o = slice(t * W5 + j * P, t * W5 + (j + 1) * P)
                            mm(b[:, j * P:(j + 1) * P], btok[r, o], uch[r, o], start=True, stop=False)
                            last = mm(b[:, j * P:(j + 1) * P], ktok[r, o], vtok[r, o], start=False, stop=True)
                    elif kind == "cy":
                        c, t, r = a[0], a[0] // 2, rows(a[0])
                        pe.wait_ge(dve_done, at("dve", "cu", c))
                        if c > 0:
                            for j in range(4):
                                mm(b[:, j * CH:(j + 1) * CH], S[c][:, j * P:(j + 1) * P],
                                   ar[:, (j * NC + c) * 128 + 64:(j * NC + c + 1) * 128], start=(j == 0), stop=False, skip_group_check=True)
                        for h in range(8):
                            vc = slice(t * W5 + h * HD, t * W5 + (h + 1) * HD)
                            o = b[64 * (h % 2):64 * (h % 2) + 64, (h // 2) * CH:(h // 2 + 1) * CH]
                            mm(o, uch[r, vc], scm[r, sco(h, t, 1)], start=(c == 0 and h < 2), stop=False, skip_group_check=True)
                            last = mm(o, vtok[r, vc], scm[r, sco(h, t, 3)], start=False, stop=(h >= 6), skip_group_check=True)
                    elif kind == "cen":
                        pe.wait_ge(act_done, at("act", "cy", NC - 1))
                        last = mm(b[:, :], centre, yt[:, a[0] * 512:(a[0] + 1) * 512], start=True, stop=True)
                    elif kind == "mt":
                        t, h = a
                        pe.wait_ge(dve_done, at("dve", "bmul", f"bB{h}"))
                        for q in range(4):
                            last = tr(b[:, q * P:(q + 1) * P], merged[:, t * D + (4 * h + q) * P:t * D + (4 * h + q + 1) * P], ident)
                    last.then_inc(pe_done, 1)

                def products(n, tokens):
                    u, k0, kn = TILES[n]
                    name, lay, _, _, width, _ = UNITS[u]
                    first, final = k0 == 0, n == LAST[u]
                    ahi, alo = (g_hi, g_lo) if name[0] == "b" else (xt_hi, xt_lo)
                    hi, lo = w_hi[:, slot(n)], w_lo[:, slot(n)]
                    if lay == "T":
                        for kk in range(kn):
                            ah, al = jt(ahi, k0 + kk), jt(alo, k0 + kk)
                            for j in range(width // P):
                                o = pbank(name, j // 2)[:, (j % 2) * SEQ:(j % 2 + 1) * SEQ]
                                cs = slice(kk * width + j * P, kk * width + (j + 1) * P)
                                mm(o, hi[:, cs], ah, start=(first and kk == 0 and j % 2 == 0), stop=False, skip_group_check=True)
                                mm(o, hi[:, cs], al, start=False, stop=False, skip_group_check=True)
                                last = mm(o, lo[:, cs], ah, start=False, stop=(final and kk == kn - 1), skip_group_check=True)
                    else:
                        for t in tokens:
                            o = pbank(name, t)[:, 0:width]
                            for kk in range(kn):
                                cs = slice(kk * width, (kk + 1) * width)
                                ah, al = jt(ahi, k0 + kk, t), jt(alo, k0 + kk, t)
                                mm(o, ah, hi[:, cs], start=(first and kk == 0), stop=False)
                                mm(o, ah, lo[:, cs], start=False, stop=False)
                                last = mm(o, al, hi[:, cs], start=False, stop=(final and kk == kn - 1))
                    return last

                for kind, *a in steps("pe", l):
                    if kind == "npart":
                        n = a[0]
                        pe.wait_ge(act_done, at("act", "nhi", n))
                        pe.wait_ge(done[nlo_on(n)], at(nlo_on(n), "nlo", n))
                        pe.wait_ge(act_done, at("act", "nxth", 0, n // 2))
                        pe.wait_ge(dve_done, at("dve", "nxtl", 0, n // 2))
                        if n == 0 and l >= 0:
                            pe.wait_ge(dve_done, at("dve", "res", 0, 0))
                        products(n, (0,)).then_inc(pe_done, 1)
                    elif kind == "tile" and a[0] < HALVED:
                        n = a[0]
                        pe.wait_ge(act_done, at("act", "nxth", 1, n // 2, back=True))
                        pe.wait_ge(dve_done, at("dve", "nxtl", 1, n // 2, back=True))
                        products(n, (1,)).then_inc(pe_done, 1)
                    elif kind == "tile" and a[0] >= NT - HALVED:
                        products(a[0], (1,)).then_inc(pe_done, 1)
                    elif kind in ("tile", "part"):
                        n = a[0]
                        u, k0, _ = TILES[n]
                        name = UNITS[u][0]
                        pe.wait_ge(act_done, at("act", "hi", n))
                        pe.wait_ge(dve_done, at("dve", "lo", n))
                        if k0 == 0 and (l or u >= 2):
                            e, m = unit_release(UNITS[(u - 2) % len(UNITS)][0])
                            pe.wait_ge(done[e], at(e, *m, back=u < 2))
                        if k0 == 0 and name[0] == "b":
                            pe.wait_ge(act_done, at("act", "ghi", name[1]))
                            pe.wait_ge(dve_done, at("dve", "glo", name[1]))
                        if name == "o0" and k0 % 4 == 0:
                            pe.wait_ge(act_done, at("act", "mth", 1, k0 // 4))
                            pe.wait_ge(dve_done, at("dve", "mtl", 1, k0 // 4))
                        products(n, (0,) if kind == "part" else (0, 1)).then_inc(pe_done, 1)
                    else:
                        fill((kind, *a))

        @block.scalar
        def _(act):
            A = nc.scalar.activation
            for l in range(-1, DEPTH):
                at = counter(l)

                def run(kind, *a):
                    m = (kind,) + a
                    if m in WIDX:
                        act.wait_ge(pe_done, at("pe", *m))
                        b = wbank(*m)
                    if kind == "hi":
                        n = a[0]
                        act.wait_ge(raw_in[n % RAW], l * (16 * NT // RAW) + 16 * (n // RAW + 1))
                        act.wait_ge(pe_done, at("pe", "tile", n - SPL))
                        return A(w_hi[:, slot(n)], raw[:, rslot(n)], ACT.Copy).then_inc(act_done, 1)
                    if kind == "nhi":
                        n = a[0]
                        act.wait_ge(raw_in[n % RAW], (l + 1) * (16 * NT // RAW) + 16)
                        if l >= 0:
                            act.wait_ge(pe_done, at("pe", "tile", NT + n - SPL))
                        return A(w_hi[:, slot(n)], raw[:, rslot(n)], ACT.Copy).then_inc(act_done, 1)
                    if kind in ("nxth", "mth"):
                        src = {"nxth": "nxt", "mth": "mt"}[kind]
                        act.wait_ge(pe_done, at("pe", src, *a))
                        return A(cut(xt_hi[:, :], a[0])[:, 4 * a[1]:4 * a[1] + 4, :], col4(wbank(src, *a)), ACT.Copy,
                                 scale=1.0 if kind == "nxth" else 0.5).then_inc(act_done, 1)
                    if kind == "vec":
                        return A(vcol[:, :], b[:, 0:NVEC], ACT.Copy).then_inc(act_done, 1)
                    if kind == "mix":
                        name = a[0]
                        act.wait_ge(pe_done, at("pe", "tile", LAST[UIDX[name]]))
                        act.wait_ge(dve_done, at("dve", "derive"))
                        if name == "zB":
                            act.wait_ge(pe_done, at("pe", "bt", "k", 1))
                        for j in range(UNITS[UIDX[name]][4] // P):
                            last = A(jt(TDST[name], j), pbank(name, j // 2)[:, (j % 2) * SEQ:(j % 2 + 1) * SEQ], ACT.Copy,
                                     scale=omu[:, MUROW[name] + j:MUROW[name] + j + 1])
                        return last.then_inc(act_done, 1)
                    if kind == "ltanh":
                        act.wait_ge(dve_done, at("dve", "shift", "lora"))
                        return A(lora[0:64, :], lora[0:64, :], ACT.Tanh).then_inc(act_done, 1)
                    if kind in ("dec", "icl"):
                        dst, hc = (ld, 0) if kind == "dec" else (iclr, 4)
                        for q in range(2):
                            j = 2 * a[0] + q
                            last = A(jt(dst, j), b[:, q * SEQ:(q + 1) * SEQ], ACT.Tanh, scale=0.5, bias=halves[:, hc + j:hc + j + 1])
                        return last.then_inc(act_done, 1)
                    if kind == "en":
                        act.wait_ge(dve_done, at("dve", "scan"))
                        return A(en[:, :], cum, ACT.Exp, scale=-1.0).then_inc(act_done, 1)
                    if kind == "ex":
                        act.wait_ge(pool_done, at("pool", "cx"))
                        return A(ld, ld, ACT.Exp).then_inc(act_done, 1)
                    if kind == "ei":
                        return A(cum, cum, ACT.Exp).then_inc(act_done, 1)
                    if kind == "ec":
                        act.wait_ge(act_done, at("act", "ei"))
                        return A(ec[:, :], cum.rearrange("p (c t) -> p c t", t=CH)[:, :, CH - 1], ACT.Copy).then_inc(act_done, 1)
                    if kind == "ksq":
                        act.wait_ge(dve_done, at("dve", "shift", "k"))
                        for j in range(4):
                            last = A(jt(b_t, j), jt(k_t, j), ACT.Square, scale=vec(KK_, j))
                        return last.then_inc(act_done, 1)
                    if kind == "nrt":
                        return A(rnt[:, :], b[0:8, 0:SEQ], ACT.Copy).then_inc(act_done, 1)
                    if kind == "vt":
                        return A(vtok[:, a[0] * W5:(a[0] + 1) * W5], b[:, :], ACT.Copy).then_inc(act_done, 1)
                    if kind == "bt":
                        act.wait_ge(dve_done, at("dve", "tt2", 1, 1))
                        return A((btok if a[0] == "b" else ktok)[:, a[1] * W5:(a[1] + 1) * W5], b[:, :], ACT.Copy).then_inc(act_done, 1)
                    if kind == "qt":
                        dst, n = (q_tr, 4) if a[0][1] == "q" else (k_tr, 2 if a[0] == "Ck" else 4)
                        return A(cut(dst[:, 0:n * SEQ], a[1]), col4(b, n), ACT.Copy).then_inc(act_done, 1)
                    if kind == "exp":
                        x_, g = a
                        t, hs = heads_of(g)
                        keys, o4 = P * (t + 1), (g % 2) * 4
                        act.wait_ge(dve_done, at("dve", "max", x_, g))
                        if x_ == "C":
                            A(esk[:, o4:o4 + len(hs)], esk[:, o4:o4 + len(hs)], ACT.Exp)
                        for i2, h in enumerate(hs):
                            o = (g % 2) * 512 + i2 * keys
                            last = A(prob[:, o:o + keys], wbank("sc", *a)[:, i2 * keys:(i2 + 1) * keys], ACT.Exp, scale=SCALE,
                                     bias=nb[:, o4 + i2:o4 + i2 + 1], accum_out=den[:, o4 + i2:o4 + i2 + 1])
                        return last.then_inc(act_done, 1)
                    if kind == "pt":
                        x_, g = a
                        if g >= 2:
                            act.wait_ge(dve_done, at("dve", "pv", x_, g - 2))
                        elif x_ == "C":
                            act.wait_ge(dve_done, at("dve", "pv", "A", g + 4))
                        return A(pT[:, (g % 2) * 512:(g % 2) * 512 + 512], b[:, :], ACT.Copy).then_inc(act_done, 1)
                    if kind == "ot":
                        return A(cut({"A": o_A, "C": o_C}[a[0]][:, :], a[1]), col4(b), ACT.Copy).then_inc(act_done, 1)
                    if kind in ("w1", "w2"):
                        if kind == "w2":
                            act.wait_ge(dve_done, at("dve", "tt1", 1, 1))
                        r = rows(a[0])
                        return A(Wb[r, a[1] * 512:(a[1] + 1) * 512], b[r, :], ACT.Copy).then_inc(act_done, 1)
                    if kind == "cp":
                        return A(pch[rows(a[0]), :], b[rows(a[0]), :], ACT.Copy).then_inc(act_done, 1)
                    if kind == "cy":
                        dst = yt[:, :].rearrange("p (j c) -> p j c", j=4)[:, :, a[0] * CH:(a[0] + 1) * CH]
                        return A(dst, b[:, 0:256].rearrange("p (j c) -> p j c", j=4), ACT.Copy).then_inc(act_done, 1)
                    if kind == "cen":
                        A(b_t[:, a[0] * 512:(a[0] + 1) * 512], b[:, :], ACT.Copy)
                        return A(ysq[:, a[0] * 512:(a[0] + 1) * 512], b[:, :], ACT.Square).then_inc(act_done, 1)
                    if kind in ("Av", "vc"):
                        name = {"Av": "Av", "vc": "Ckv"}[kind]
                        act.wait_ge(pe_done, at("pe", "tile", LAST[UIDX[name]]))
                        dst, w = (v_a, W5) if kind == "Av" else (v_c, P)
                        for t in range(2):
                            src = pbank(name, t)[:, :] if kind == "Av" else pbank(name, t)[:, P:2 * P]
                            last = A(dst[:, t * w:(t + 1) * w], src, ACT.Copy)
                        return last.then_inc(act_done, 1)
                    if kind == "ztanh":
                        name = "z" + a[0]
                        act.wait_ge(pe_done, at("pe", "tile", LAST[UIDX[name]]))
                        if a[0] == "A":
                            act.wait_ge(dve_done, at("dve", "kb"))
                            act.wait_ge(pool_done, at("pool", "kt"))
                        else:
                            act.wait_ge(dve_done, at("dve", "glo", {"C": "A", "B": "C"}[a[0]]))
                        if a[0] == "B":
                            act.wait_ge(dve_done, at("dve", "shift", "zB"))
                        for t in range(2):
                            last = A(sz[:, t * 512:(t + 1) * 512], z_part(a[0], t), ACT.Tanh, scale=0.5)
                        return last.then_inc(act_done, 1)
                    if kind == "gate":
                        name, c = a[0], int(a[0][2])
                        act.wait_ge(pe_done, at("pe", "tile", LAST[UIDX[name]]))
                        if name[1] == "A":
                            act.wait_ge(dve_done, at("dve", "rs", 1, 1, 1))
                        else:
                            act.wait_ge(dve_done, at("dve", "bmul", "b" + {"C": "A", "B": "C"}[name[1]] + name[2]))
                        for t in range(2):
                            last = A(gate[:, t * D + c * 512:t * D + (c + 1) * 512], pbank(name, t)[:, :], ACT.Tanh, scale=0.5)
                        return last.then_inc(act_done, 1)
                    if kind == "ghi":
                        act.wait_ge(dve_done, at("dve", "g", a[0]))
                        if a[0] != "A":
                            act.wait_ge(pe_done, at("pe", "tile", LAST[UIDX["b" + {"C": "A", "B": "C"}[a[0]] + "1"]]))
                        return A(g_hi[:, :], sz[:, :], ACT.Copy).then_inc(act_done, 1)
                    raise ValueError(kind)

                for i, m in enumerate(steps("act", l)):
                    if START["act", l] + i and m[0] not in ("hi", "nhi"):
                        act.wait_ge(act_done, START["act", l] + i)
                    run(*m)
                if l >= 0:
                    continue
                act.wait_ge(cst_in, 16)
                A(id_bf[:, :], ident, ACT.Copy).then_inc(bf_ready, 1)
                A(neg_bf[:, :], cst[:, C_NEG:C_NEG + 256], ACT.Copy).then_inc(bf_ready, 1)
                act.wait_ge(angles_ready, 1)
                for t in range(2):
                    r = rot[:, t * 128:(t + 1) * 128].rearrange("p (f two d) -> p f two d", f=2, two=2)
                    sn, cs = ang[:, t * 32:(t + 1) * 32], ang[:, 64 + t * 32:64 + (t + 1) * 32]
                    A(r[:, 0, 0, :], cs, ACT.Sin)
                    A(r[:, 0, 1, :], cs, ACT.Sin)
                    A(r[:, 1, 0, :], sn, ACT.Sin, scale=-1.0)
                    last = A(r[:, 1, 1, :], sn, ACT.Sin)
                last.then_inc(rot_ready, 1)

        @block.vector
        def _(dve):
            tt, ts, stt = nc.vector.tensor_tensor, nc.vector.tensor_scalar, nc.vector.scalar_tensor_tensor
            for l in range(-1, DEPTH):
                at = counter(l)
                link, links = linker("dve", l)

                def run(kind, *a):
                    m = (kind,) + a
                    if m in WIDX:
                        dve.wait_ge(pe_done, at("pe", *m))
                        b = wbank(*m)
                    if kind == "lo":
                        n = a[0]
                        dve.wait_ge(act_done, at("act", "hi", n))
                        return tt(w_lo[:, slot(n)], raw[:, rslot(n)], w_hi[:, slot(n)].bitcast(f32), ALU.subtract).then_inc(dve_done, 1)
                    if kind == "nlo":
                        n = a[0]
                        dve.wait_ge(act_done, at("act", "nhi", n))
                        return tt(w_lo[:, slot(n)], raw[:, rslot(n)], w_hi[:, slot(n)].bitcast(f32), ALU.subtract).then_inc(dve_done, 1)
                    if kind == "nxtl":
                        dve.wait_ge(act_done, at("act", "nxth", *a))
                        half = lambda buf: cut(buf, a[0])[:, 4 * a[1]:4 * a[1] + 4, :]
                        return tt(half(xt_lo[:, :]), col4(wbank("nxt", *a)), half(xt_hi[:, :].bitcast(f32)), ALU.subtract).then_inc(dve_done, 1)
                    if kind == "mtl":
                        dve.wait_ge(act_done, at("act", "mth", *a))
                        half = lambda buf: cut(buf, a[0])[:, 4 * a[1]:4 * a[1] + 4, :]
                        return stt(half(xt_lo[:, :]), col4(wbank("mt", *a)), 0.5, half(xt_hi[:, :].bitcast(f32)), ALU.mult, ALU.subtract).then_inc(dve_done, 1)
                    if kind == "derive":
                        dve.wait_ge(act_done, at("act", "vec"))
                        dve.wait_ge(sink_in, l * 16 + 16)
                        ts(omu[:, :], vcol[:, MU:MU + 17], -1.0, 1.0, ALU.mult, ALU.add)
                        ts(halves[:, 0:8], vcol[:, W0:W0 + 8], 0.5, None, ALU.mult)
                        ts(halves[:, 8:12], vcol[:, KA:KA + 4], 0.5, None, ALU.mult)
                        for j in range(4):
                            ts(bor[:, j * P:(j + 1) * P], head_ones, vec(RK_, j), None, ALU.mult)
                        return ts(nsink[:, :], sink[:, :], -1.0, None, ALU.mult).then_inc(dve_done, 1)
                    if kind == "shift":
                        name = a[0]
                        dve.wait_ge(act_done, at("act", "mix", name))
                        for j in range(UNITS[UIDX[name]][4] // P):
                            o = jt(TDST[name], j)[:, 1:SEQ]
                            h = pbank(name, j // 2)[:, (j % 2) * SEQ:(j % 2) * SEQ + SEQ - 1]
                            last = stt(o, h, vec(MUROW[name], j), o, ALU.mult, ALU.add)
                        return last.then_inc(dve_done, 1)
                    if kind == "ld":
                        dve.wait_ge(act_done, at("act", "dec", 1))
                        return ts(ld, ld, -DECAY_SCALE / 2, -DECAY_SCALE / 2, ALU.mult, ALU.add).then_inc(dve_done, 1)
                    if kind == "scan":
                        dve.wait_ge(dve_done, at("dve", "ld"))
                        for j in range(4):
                            last = nc.vector.tensor_tensor_scan(jt(cum, j), cst[:, C_RST:C_RST + SEQ], jt(ld, j), 0.0, ALU.mult, ALU.add)
                        return last.then_inc(dve_done, 1)
                    if kind == "ta":
                        dve.wait_ge(act_done, at("act", "icl", 1))
                        for j in range(4):
                            last = ts(jt(tmp, j), jt(iclr, j), 1.0, halves[:, 8 + j:9 + j], ALU.subtract, ALU.mult)
                        last.then_inc(dve_chain, 1)
                        dve.wait_ge(dve_chain, link())
                        return ts(iclr, iclr, 0.5, 0.5, ALU.mult, ALU.add).then_inc(dve_done, 1)
                    if kind == "nss":
                        if a[0] == "k":
                            return ts(ss[:, :], b[:, 0:16], 1e-24, None, ALU.max).then_inc(dve_done, 1)
                        return ts(ss[:, :], b[:, 0:16], 1.0 / HD, GN_EPS, ALU.mult, ALU.add).then_inc(dve_done, 1)
                    if kind == "nrb":
                        if a[0] == "k":
                            for q in range(2):
                                j = 2 * a[1] + q
                                last = stt(jt(b_t, j), jt(k_t, j), vec(KK_, j), b[:, q * SEQ:(q + 1) * SEQ], ALU.mult, ALU.mult)
                            return last.then_inc(dve_done, 1)
                        o = b_t[:, a[1] * 512:(a[1] + 1) * 512]
                        return tt(o, o, b[:, :], ALU.mult).then_inc(dve_done, 1)
                    if kind == "k2":
                        dve.wait_ge(dve_done, at("dve", "nrb", "k", 1))
                        return stt(k_t[:, :], tmp[:, :], 1.0, k_t[:, :], ALU.add, ALU.mult).then_inc(dve_done, 1)
                    if kind == "ara":
                        dve.wait_ge(act_done, at("act", "ex"))
                        o = ar[:, :].rearrange("p (n two t) -> p n two t", two=2, t=CH)[:, :, 0, :]
                        return stt(o, b_t[:, :].rearrange("p (n t) -> p n t", t=CH), -1.0, ld.rearrange("p (n t) -> p n t", t=CH),
                                   ALU.mult, ALU.mult).then_inc(dve_done, 1)
                    if kind == "kb":
                        tt(b_t[:, :], b_t[:, :], iclr, ALU.mult).then_inc(dve_chain, 1)
                        dve.wait_ge(dve_chain, link())
                        dve.wait_ge(act_done, at("act", "en"))
                        return tt(b_t[:, :], b_t[:, :], en[:, :], ALU.mult).then_inc(dve_done, 1)
                    if kind == "bon":
                        dve.wait_ge(act_done, at("act", "vt", 1))
                        o = v_t[:, a[0] * 512:(a[0] + 1) * 512]
                        tt(o, o, b[:, :], ALU.mult).then_inc(dve_chain, 1)
                        dve.wait_ge(dve_chain, link())
                        for j in (2 * a[0], 2 * a[0] + 1):
                            last = ts(jt(v_t, j), jt(v_t, j), vec(GB, j), None, ALU.add)
                        return last.then_inc(dve_done, 1)
                    if kind in ("rope", "ropek"):
                        name, t = (a[0], a[1]) if kind == "rope" else ("Ckv", a[0])
                        n = H if kind == "rope" else 2
                        dve.wait_ge(pe_done, at("pe", "tile", LAST[UIDX[name]]))
                        if name == "Ak":
                            dve.wait_ge(act_done, at("act", "qt", "Aq", t))
                        elif name == "Cq":
                            dve.wait_ge(act_done, at("act", "qt", "Ak", t))
                        elif name == "Ckv":
                            dve.wait_ge(act_done, at("act", "vc"))
                        src = pbank(name, t)[:, 0:n * HD]
                        if kind == "rope":
                            o = roped[:, t * W5:(t + 1) * W5].rearrange("p (n d) -> p n d", d=HD)
                        else:
                            kd = kdup[:, t * 256:(t + 1) * 256].rearrange("p (n two d) -> p n two d", two=2, d=HD)
                            o = kd[:, :, 0, :]
                        cos2 = rot[:, t * 128:t * 128 + 64].unsqueeze(1).to_broadcast([P, n, HD])
                        sin2 = rot[:, t * 128 + 64:(t + 1) * 128].rearrange("p (two d) -> p two d", two=2).unsqueeze(1).to_broadcast([P, n, 2, 32])
                        sw = rswap[:, 0:n * HD].rearrange("p (n two d) -> p n two d", two=2, d=32)
                        tt(o, src.rearrange("p (n d) -> p n d", d=HD), cos2, ALU.mult)
                        tt(sw, src.rearrange("p (n two d) -> p n two d", two=2, d=32)[:, :, ::-1, :], sin2, ALU.mult).then_inc(dve_chain, 1)
                        dve.wait_ge(dve_chain, link())
                        last = tt(o, o, rswap[:, 0:n * HD].rearrange("p (n d) -> p n d", d=HD), ALU.add)
                        if kind == "ropek":
                            last.then_inc(dve_chain, 1)
                            dve.wait_ge(dve_chain, link())
                            last = nc.vector.tensor_copy(kd[:, :, 1, :], kd[:, :, 0, :])
                        return last.then_inc(dve_done, 1)
                    if kind == "max":
                        x_, g = a
                        t, hs = heads_of(g)
                        n, o4 = len(hs), (g % 2) * 4
                        dve.wait_ge(pe_done, at("pe", "sc", *a))
                        if g >= 2:
                            dve.wait_ge(act_done, at("act", "exp", x_, g - 2))
                        elif x_ == "C":
                            dve.wait_ge(act_done, at("act", "exp", "A", g + 4))
                        nc.vector.reduce_max(mx[:, o4:o4 + n], wbank("sc", *a)[:, :].rearrange("p (n k) -> p n k", n=n), AX.X).then_inc(dve_chain, 1)
                        dve.wait_ge(dve_chain, link())
                        if x_ == "A":
                            return ts(nb[:, o4:o4 + n], mx[:, o4:o4 + n], -SCALE, None, ALU.mult).then_inc(dve_done, 1)
                        if g >= 2:
                            dve.wait_ge(dve_done, at("dve", "pv", x_, g - 2))
                        sk = slice(hs[0], hs[-1] + 1, 2)
                        stt(nb[:, o4:o4 + n], mx[:, o4:o4 + n], -SCALE, nsink[:, sk], ALU.mult, ALU.min).then_inc(dve_chain, 1)
                        dve.wait_ge(dve_chain, link())
                        return tt(esk[:, o4:o4 + n], sink[:, sk], nb[:, o4:o4 + n], ALU.add).then_inc(dve_done, 1)
                    if kind == "pv":
                        x_, g = a
                        t, hs = heads_of(g)
                        n, o4 = len(hs), (g % 2) * 4
                        dve.wait_ge(act_done, at("act", "exp", x_, g))
                        if x_ == "C":
                            tt(den[:, o4:o4 + n], den[:, o4:o4 + n], esk[:, o4:o4 + n], ALU.add).then_inc(dve_chain, 1)
                            dve.wait_ge(dve_chain, link())
                        nc.vector.reciprocal(rec[:, o4:o4 + n], den[:, o4:o4 + n]).then_inc(dve_chain, 1)
                        dve.wait_ge(dve_chain, link())
                        if g >= 2:
                            dve.wait_ge(act_done, at("act", "ot", x_, 0))
                        elif x_ == "C":
                            dve.wait_ge(act_done, at("act", "ot", "A", 1))
                        o = otok[:, :].rearrange("p (q two d) -> p q two d", two=2, d=HD)[:, hs[0] // 2:hs[0] // 2 + n, hs[0] % 2, :]
                        return tt(o, b[:, 0:n * HD].rearrange("p (n d) -> p n d", d=HD),
                                  rec[:, o4:o4 + n].unsqueeze(2).to_broadcast([P, n, HD]), ALU.mult).then_inc(dve_done, 1)
                    if kind == "rs":
                        t, par, half = a
                        o = scm[:, ((t * 2 + par) * 4 + 2 * half) * 256:((t * 2 + par) * 4 + 2 * half + 2) * 256]
                        return tt(o.rearrange("p (n c) -> p n c", c=P), b[:, :].rearrange("p (n c) -> p n c", c=P),
                                  cst[:, C_MSK:C_MSK + P].unsqueeze(1).to_broadcast([P, 4, P]), ALU.mult).then_inc(dve_done, 1)
                    if kind == "sub":
                        if a[0] == 0:
                            dve.wait_ge(lb_in, l * 16 + 16)
                            nc.vector.tensor_copy(X, cst[:, C_EYE16:C_EYE16 + 256]).then_inc(dve_chain, 1)
                            dve.wait_ge(dve_chain, link())
                        else:
                            dve.wait_ge(dve_done, at("dve", "sub", a[0] - 1))
                        x3, l3 = X.rearrange("p (t c) -> p t c", c=16), lb.rearrange("p (s t) -> p s t", t=16)
                        for s in range(5 * a[0], 5 * a[0] + 5):
                            n, c = 15 - s, s + 1
                            pr = subt[:, 0:n * c].rearrange("p (t c) -> p t c", c=c)
                            tt(pr, l3[:, s, s + 1:16].unsqueeze(2).to_broadcast([P, n, c]),
                                    x3[:, s, 0:c].unsqueeze(1).to_broadcast([P, n, c]), ALU.mult).then_inc(dve_chain, 1)
                            dve.wait_ge(dve_chain, link())
                            last = tt(x3[:, s + 1:16, 0:c], x3[:, s + 1:16, 0:c], pr, ALU.add)
                            if s < 5 * a[0] + 4:
                                last.then_inc(dve_chain, 1)
                                dve.wait_ge(dve_chain, link())
                        if a[0] == 2:
                            last.then_inc(dve_chain, 1)
                            dve.wait_ge(dve_chain, link())
                            last = nc.vector.tensor_copy(XT.rearrange("p (c t) -> p c t", t=16), X.rearrange("p (t c) -> p c t", c=16))
                        return last.then_inc(dve_done, 1)
                    if kind in ("t1", "tt1", "tt2"):
                        dst = T if kind == "t1" else TT
                        o = dst[rows(a[0]), a[1] * 512:(a[1] + 1) * 512]
                        return tt(o, o, b[rows(a[0]), :], ALU.add).then_inc(dve_done, 1)
                    if kind == "cu":
                        c = a[0]
                        return nc.vector.tensor_copy(uch[rows(c), (c // 2) * W5:(c // 2 + 1) * W5], b[rows(c), :]).then_inc(dve_done, 1)
                    if kind == "cs":
                        c = a[0]
                        dve.wait_ge(pool_done, at("pool", "states"))
                        for p_ in range(2):
                            r = slice(64 * p_, 64 * p_ + 64)
                            blk = lambda buf: buf[r, :].rearrange("p (j two v) -> p j two v", two=2, v=HD)[:, :, p_, :]
                            e = ec[r, :].rearrange("p (j c) -> p j c", c=NC)[:, :, c].unsqueeze(2).to_broadcast([64, 4, HD])
                            if c == 0:
                                last = tt(blk(S[1]), blk(b), e, ALU.mult)
                            else:
                                tt(blk(S[c + 1]), blk(b), blk(S[c]), ALU.add).then_inc(dve_chain, 1)
                                dve.wait_ge(dve_chain, link())
                                last = tt(blk(S[c + 1]), blk(S[c + 1]), e, ALU.mult)
                        return last.then_inc(dve_done, 1)
                    if kind == "gn":
                        dve.wait_ge(dve_done, at("dve", "nrb", "y", 1))
                        for j in range(4):
                            last = stt(jt(v_t, j), jt(b_t, j), vec(GG, j), jt(v_t, j), ALU.mult, ALU.add)
                        return last.then_inc(dve_done, 1)
                    if kind == "sz":
                        dve.wait_ge(act_done, at("act", "ztanh", a[0]))
                        for t in range(2):
                            o = sz[:, t * 512:(t + 1) * 512]
                            last = stt(o, o, 1.0, z_part(a[0], t), ALU.add, ALU.mult)
                        return last.then_inc(dve_done, 1)
                    if kind == "g":
                        dve.wait_ge(dve_done, at("dve", "sz", a[0]))
                        if a[0] == "B":
                            dve.wait_ge(dve_done, at("dve", "gn"))
                        else:
                            dve.wait_ge(act_done, at("act", "ot", a[0], 1))
                        return stt(sz[:, :], {"A": o_A, "C": o_C, "B": v_t}[a[0]][:, :], 0.5, sz[:, :], ALU.mult, ALU.mult).then_inc(dve_done, 1)
                    if kind == "glo":
                        dve.wait_ge(act_done, at("act", "ghi", a[0]))
                        return tt(g_lo[:, :], sz[:, :], g_hi[:, :].bitcast(f32), ALU.subtract).then_inc(dve_done, 1)
                    if kind == "bmul":
                        name, c = a[0], int(a[0][2])
                        dve.wait_ge(pe_done, at("pe", "tile", LAST[UIDX[name]]))
                        dve.wait_ge(act_done, at("act", "gate", "G" + name[1:]))
                        if name[1] != "A" and name != "bC0":
                            dve.wait_ge(pool_done, at("pool", "add" + {"bC1": "C0", "bB0": "C1", "bB1": "C1"}[name]))
                        for t in range(2):
                            cols = slice(t * D + c * 512, t * D + (c + 1) * 512)
                            o = merged[:, cols] if name[1] == "A" else tmp[:, t * 512:(t + 1) * 512]
                            last = stt(o, gate[:, cols], 1.0, pbank(name, t)[:, :], ALU.add, ALU.mult)
                        if name[1] == "B":
                            last.then_inc(dve_chain, 1)
                            dve.wait_ge(dve_chain, link())
                            halves2 = merged[:, :].rearrange("p (t c) -> p t c", t=2)[:, :, c * 512:(c + 1) * 512]
                            last = tt(halves2, halves2, tmp[:, :].rearrange("p (t c) -> p t c", t=2), ALU.add)
                        return last.then_inc(dve_done, 1)
                    if kind == "res":
                        c, t = a
                        dve.wait_ge(pe_done, at("pe", "part" if t == 0 else "tile", LAST[UIDX[f"o{c}"]]))
                        o = xres[:, t * D + c * 512:t * D + (c + 1) * 512]
                        stt(o, o, ALPHA, pbank(f"o{c}", t)[:, :], ALU.mult, ALU.add).then_inc(dve_chain, 1)
                        dve.wait_ge(dve_chain, link())
                        return nc.vector.bn_stats(stat[:, (2 * t + c) * 6:(2 * t + c + 1) * 6], o).then_inc(dve_done, 1)
                    if kind == "agg":
                        t = a[0]
                        nc.vector.bn_aggr(agg[:, 2 * t:2 * t + 2], stat[:, t * 12:(t + 1) * 12]).then_inc(dve_chain, 1)
                        dve.wait_ge(dve_chain, link())
                        return ts(rstd[:, t:t + 1], agg[:, 2 * t + 1:2 * t + 2], LN_EPS, None, ALU.add).then_inc(dve_done, 1)
                    if kind == "norm":
                        t, h = a
                        dve.wait_ge(pool_done, at("pool", "rstd", t))
                        dve.wait_ge(ln_in, l * 32 + 32)
                        o = xres[:, t * D + h * 512:t * D + (h + 1) * 512]
                        stt(o, o, agg[:, 2 * t:2 * t + 1], lnp[:, h * 512:(h + 1) * 512], ALU.subtract, ALU.mult).then_inc(dve_chain, 1)
                        dve.wait_ge(dve_chain, link())
                        return stt(o, o, rstd[:, t:t + 1], lnp[:, D + h * 512:D + (h + 1) * 512], ALU.mult, ALU.add).then_inc(dve_done, 1)
                    raise ValueError(kind)

                for i, m in enumerate(steps("dve", l)):
                    if START["dve", l] + i and m[0] not in ("lo", "nlo"):
                        dve.wait_ge(dve_done, START["dve", l] + i)
                    run(*m)
                assert links[0] == (LINKS["dve"] if l >= 0 else 0), links
                if l >= 0:
                    continue
                pre = [0]

                def then(ins):
                    pre[0] += 1
                    ins.then_inc(pos_ready, 1)
                    dve.wait_ge(pos_ready, pre[0])

                dve.wait_ge(cst_in, 16)
                dve.wait_ge(pos_in, 32)
                then(nc.vector.tensor_copy(pos_f[:, :], pos_i[:, :]))
                for f in range(2):
                    for t in range(2):
                        o = ang[:, f * 64 + t * 32:f * 64 + (t + 1) * 32]
                        last = ts(o, cst[:, C_INV:C_INV + 32], pos_f[:, t:t + 1], None, ALU.mult)
                then(last)
                for f in range(2):
                    last = ts(turn[:, f * 64:(f + 1) * 64], ang[:, f * 64:(f + 1) * 64], 1 / (2 * math.pi), 0.25 * f, ALU.mult, ALU.add)
                then(last)
                then(ts(turn[:, :], turn[:, :], ROUND, None, ALU.add))
                then(ts(turn[:, :], turn[:, :], ROUND, None, ALU.subtract))
                for c in TWO_PI:
                    then(stt(ang[:, :], turn[:, :], -c, ang[:, :], ALU.mult, ALU.add))
                then(ts(ang[:, 64:128], ang[:, 64:128], math.pi / 2, None, ALU.add))
                ts(ang[:, :], ang[:, :], PI_MAX, -PI_MAX, ALU.min, ALU.max).then_inc(angles_ready, 1)
                nc.vector.memset(mhalf[:, :], -0.5)
                dve.wait_ge(rot_ready, 1)

        @block.gpsimd
        def _(pool):
            tt = nc.gpsimd.tensor_tensor
            for l in range(-1, DEPTH):
                at = counter(l)
                link, links = linker("pool", l)

                def run(kind, *a):
                    if kind == "zero":
                        if l:
                            pool.wait_ge(dve_done, at("dve", "norm", 1, 1, back=True))
                        nc.gpsimd.memset(T[:, :], 0.0).then_inc(pool_chain, 1)
                        pool.wait_ge(pool_chain, link())
                        return nc.gpsimd.memset(TT[:, :], 0.0).then_inc(pool_done, 1)
                    if kind == "cx":
                        pool.wait_ge(dve_done, at("dve", "scan"))
                        return tt(ld, cum, ld, ALU.subtract).then_inc(pool_done, 1)
                    if kind in ("rnk", "rny"):
                        pool.wait_ge(dve_done, at("dve", "nss", kind[2]))
                        return tt(rn[:, :], ss[:, :], mhalf[:, :], ALU.pow).then_inc(pool_done, 1)
                    if kind == "arr":
                        pool.wait_ge(act_done, at("act", "ei"))
                        pool.wait_ge(dve_done, at("dve", "shift", "r"))
                        o = ar[:, :].rearrange("p (n two t) -> p n two t", two=2, t=CH)[:, :, 1, :]
                        return tt(o, r_t.rearrange("p (n t) -> p n t", t=CH), cum.rearrange("p (n t) -> p n t", t=CH), ALU.mult).then_inc(pool_done, 1)
                    if kind == "rk":
                        pool.wait_ge(dve_done, at("dve", "k2"))
                        return tt(tmp[:, :], r_t, k_t[:, :], ALU.mult).then_inc(pool_done, 1)
                    if kind == "kt":
                        pool.wait_ge(act_done, at("act", "en"))
                        pool.wait_ge(pool_done, at("pool", "rk"))
                        return tt(k_t[:, :], k_t[:, :], en[:, :], ALU.mult).then_inc(pool_done, 1)
                    if kind in ("lm1", "lm2"):
                        if kind == "lm1":
                            pool.wait_ge(dve_done, at("dve", "rs", 1, 1, 1))
                            if l:
                                pool.wait_ge(dve_done, at("dve", "norm", 1, 1, back=True))
                        else:
                            pool.wait_ge(act_done, at("act", "w1", 1, 1))
                        mask = cst[:, (C_M16 if kind == "lm1" else C_M32):(C_M16 if kind == "lm1" else C_M32) + CH]
                        return tt(LM[:, :].rearrange("p (n c) -> p n c", c=CH), scm[:, :].rearrange("p (n c) -> p n c", c=256)[:, :, 0:CH],
                                  mask.unsqueeze(1).to_broadcast([P, 16, CH]), ALU.mult).then_inc(pool_done, 1)
                    if kind == "states":
                        pool.wait_ge(pe_done, at("pe", "sc", "C", 5))
                        nc.gpsimd.memset(q_tr[:, :], 0.0)
                        return nc.gpsimd.memset(k_tr[:, 0:512], 0.0).then_inc(pool_done, 1)
                    if kind == "rstd":
                        pool.wait_ge(dve_done, at("dve", "agg", a[0]))
                        return tt(rstd[:, a[0]:a[0] + 1], rstd[:, a[0]:a[0] + 1], mhalf[:, 0:1], ALU.pow).then_inc(pool_done, 1)
                    if kind == "nlo":
                        n = a[0]
                        pool.wait_ge(act_done, at("act", "nhi", n))
                        return tt(w_lo[:, slot(n)], raw[:, rslot(n)], w_hi[:, slot(n)].bitcast(f32), ALU.subtract).then_inc(pool_done, 1)
                    c = int(kind[4])
                    pool.wait_ge(dve_done, at("dve", "bmul", "b" + kind[3:]))
                    for t in range(2):
                        o = merged[:, t * D + c * 512:t * D + (c + 1) * 512]
                        last = tt(o, o, tmp[:, t * 512:(t + 1) * 512], ALU.add)
                    return last.then_inc(pool_done, 1)

                for i, m in enumerate(steps("pool", l)):
                    if START["pool", l] + i and m[0] != "nlo":
                        pool.wait_ge(pool_done, START["pool", l] + i)
                    run(*m)
                assert links[0] == (LINKS["pool"] if l >= 0 else 0), links


def kernel(**inputs):
    import concourse.bacc as bacc
    from concourse.bass_utils import run_bass_kernel_spmd

    nc = bacc.Bacc("TRN2", target_bir_lowering=False, num_devices=1, dynamic_dma_scratch_size=1024)
    arrays, args = {}, []
    for name in INPUTS:
        a = np.ascontiguousarray(constants() if name == "consts" else inputs[name])
        arrays[f"in_{name}"] = a
        args.append(nc.dram_tensor(f"in_{name}", a.shape, mybir.dt.from_np(a.dtype), kind="ExternalInput").ap())
    args.append(nc.dram_tensor("out_x", (1, SEQ, D), mybir.dt.float32, kind="ExternalOutput").ap())
    hybrid_trunk(nc, *args)
    r = run_bass_kernel_spmd(nc, [arrays], core_ids=[0])
    return r.results[0]["out_x"]
```
